# Optimizing a Trainium2 kernel written in Bass

```python
import math
import jax, jax.numpy as jnp
from jax import lax
import numpy as np

D_MODEL = 1024
BATCH = 1
SEQ = 512
DEPTH = 1

CHUNK = 64
D_MIX = D_MODEL

HG_HEADS = 4
HG_DK = 128
HG_DV = 128
HG_WIDTH = HG_HEADS * HG_DV

AT_HEADS = 8
AT_DH = 64
AT_WIDTH = AT_HEADS * AT_DH
Q_RANK = 256
KV_RANK = 128
IDX_HEADS = 4
IDX_DH = 64
TOPK_MAX = 256

IN_SIZES = (
    HG_HEADS * HG_DK,
    HG_HEADS * HG_DK,
    HG_HEADS * HG_DV,
    HG_HEADS * HG_DV,
    Q_RANK,
    KV_RANK,
    IDX_DH,
    IDX_HEADS,
)
D_IN = sum(IN_SIZES)
IN_SPLITS = tuple(int(v) for v in np.cumsum(IN_SIZES)[:-1])

N_EXPERTS = 64
TOP_K = 8
N_GROUPS = 8
TOPK_GROUPS = 4
D_EXPERT = 256
D_SHARED = 256
ROUTED_SCALE = 2.5

ALPHA = (2.0 * DEPTH) ** 0.25
BETA = (8.0 * DEPTH) ** -0.25
LN_EPS = 1e-5
RMS_EPS = 1e-6

kernel_name = "hybrid_hgrn2_dsa_moe_deepnorm"

def layer_norm(x, g, b):
    xf = x.astype(jnp.float32)
    mu = jnp.mean(xf, axis=-1, keepdims=True)
    var = jnp.mean(jnp.square(xf - mu), axis=-1, keepdims=True)
    return ((xf - mu) * lax.rsqrt(var + LN_EPS) * g + b).astype(x.dtype)

def rms_norm(x, g):
    xf = x.astype(jnp.float32)
    return xf * lax.rsqrt(jnp.mean(jnp.square(xf), axis=-1, keepdims=True) + RMS_EPS) * g

def alibi_slopes(n_heads):
    return jnp.exp2(-8.0 * (jnp.arange(n_heads, dtype=jnp.float32) + 1.0) / n_heads)

def hgrn2_mixer(q, f_logit, inp, gate, lb, norm_g):
    B, S, _ = q.shape
    n_c = S // CHUNK

    def heads(t, d):
        return t.reshape(B, n_c, CHUNK, HG_HEADS, d).transpose(0, 3, 1, 2, 4)

    qf = jax.nn.silu(q.astype(jnp.float32))
    f = lb + (1.0 - lb) * jax.nn.sigmoid(f_logit.astype(jnp.float32))
    kf = 1.0 - f
    qh, kh, lfh = heads(qf, HG_DK), heads(kf, HG_DK), heads(jnp.log(f), HG_DK)
    vh = heads(inp.astype(jnp.float32), HG_DV)

    b = jnp.cumsum(lfh, axis=3)
    b_last = b[:, :, :, -1:, :]
    q_dec = qh * jnp.exp(b)
    k_inv = kh * jnp.exp(-b)

    causal = jnp.tril(jnp.ones((CHUNK, CHUNK), dtype=bool))
    scores = jnp.where(causal, jnp.einsum('bhncd,bhnsd->bhncs', q_dec, k_inv), 0.0)
    o_intra = jnp.einsum('bhncs,bhnsv->bhncv', scores, vh)

    d_state = jnp.einsum('bhncd,bhncv->bhndv', kh * jnp.exp(b_last - b), vh)
    chunk_decay = jnp.exp(b_last[:, :, :, 0, :])

    def step(state, xs):
        ds, dec = xs
        return dec[..., None] * state + ds, state

    s0 = jnp.zeros((B, HG_HEADS, HG_DK, HG_DV), jnp.float32)
    _, s_prev = lax.scan(step, s0, (jnp.moveaxis(d_state, 2, 0), jnp.moveaxis(chunk_decay, 2, 0)))
    s_prev = jnp.moveaxis(s_prev, 0, 2)
    o_inter = jnp.einsum('bhncd,bhndv->bhncv', q_dec, s_prev)

    o = (o_intra + o_inter).transpose(0, 2, 3, 1, 4).reshape(B, S, HG_HEADS, HG_DV)
    o = rms_norm(o, norm_g) * jax.nn.silu(gate.astype(jnp.float32).reshape(B, S, HG_HEADS, HG_DV))
    return o.reshape(B, S, HG_WIDTH)

def dsa_mixer(c_q, c_kv, k_idx_raw, w_idx, q_norm_g, w_q_up, w_qidx_up, kv_norm_g, w_kv_up,
              idx_ln_g, idx_ln_b):
    B, S, _ = c_q.shape
    dt = c_q.dtype
    cq = rms_norm(c_q, q_norm_g).astype(dt)
    q = (cq @ w_q_up).reshape(B, S, AT_HEADS, AT_DH)
    q_idx = (cq @ w_qidx_up).reshape(B, S, IDX_HEADS, IDX_DH)
    ckv = rms_norm(c_kv, kv_norm_g).astype(dt)
    kv = ckv @ w_kv_up
    k = kv[..., :AT_WIDTH].reshape(B, S, AT_HEADS, AT_DH)
    v = kv[..., AT_WIDTH:].reshape(B, S, AT_HEADS, AT_DH)
    k_idx = layer_norm(k_idx_raw, idx_ln_g, idx_ln_b)
    w_heads = w_idx.astype(jnp.float32) * (IDX_HEADS ** -0.5) * (IDX_DH ** -0.5)

    k_top = min(TOPK_MAX, S // 4)
    slopes = alibi_slopes(AT_HEADS)
    scale = AT_DH ** -0.5
    key_pos = jnp.arange(S)

    def block(c):
        start = c * CHUNK
        end = start + CHUNK
        qb = lax.dynamic_slice_in_dim(q, start, CHUNK, axis=1)
        qib = lax.dynamic_slice_in_dim(q_idx, start, CHUNK, axis=1)
        wb = lax.dynamic_slice_in_dim(w_heads, start, CHUNK, axis=1)
        logits = jnp.einsum('bcid,bsd->bcis', qib, k_idx, preferred_element_type=jnp.float32)
        idx_score = jnp.einsum('bci,bcis->bcs', wb, jax.nn.relu(logits))
        idx_score = jnp.where(key_pos < end, idx_score, -jnp.inf)
        _, sel = lax.top_k(idx_score, k_top)
        k_sel = jax.vmap(lambda kk, ii: kk[ii])(k, sel)
        v_sel = jax.vmap(lambda vv, ii: vv[ii])(v, sel)
        s = jnp.einsum('bchd,bckhd->bchk', qb, k_sel, preferred_element_type=jnp.float32) * scale
        q_pos = start + jnp.arange(CHUNK)
        dist = jnp.abs(q_pos[None, :, None] - sel).astype(jnp.float32)
        s = s - slopes[None, None, :, None] * dist[:, :, None, :]
        s = jnp.where((sel < end)[:, :, None, :], s, -jnp.inf)
        p = jax.nn.softmax(s, axis=-1)
        return jnp.einsum('bchk,bckhd->bchd', p, v_sel.astype(jnp.float32))

    out = lax.map(block, jnp.arange(S // CHUNK))
    return out.transpose(1, 0, 2, 3, 4).reshape(B, S, AT_WIDTH)

def moe_ffn(x, w_router, router_bias, w_e_gate, w_e_up, w_e_down, w_s_gate, w_s_up, w_s_down):
    B, S, D = x.shape
    t = x.reshape(-1, D)
    T = t.shape[0]
    scores = jax.nn.sigmoid((t @ w_router).astype(jnp.float32))
    sel_scores = scores + router_bias.astype(jnp.float32)
    per_group = N_EXPERTS // N_GROUPS
    grp_score = lax.top_k(sel_scores.reshape(T, N_GROUPS, per_group), 2)[0].sum(-1)
    _, g_idx = lax.top_k(grp_score, TOPK_GROUPS)
    g_mask = jnp.any(g_idx[..., None] == jnp.arange(N_GROUPS), axis=1)
    e_mask = jnp.repeat(g_mask, per_group, axis=1)
    _, e_idx = lax.top_k(jnp.where(e_mask, sel_scores, -jnp.inf), TOP_K)
    w = jnp.take_along_axis(scores, e_idx, axis=1)
    w = w / jnp.sum(w, axis=-1, keepdims=True) * ROUTED_SCALE
    gates = jnp.zeros((T, N_EXPERTS), jnp.float32).at[jnp.arange(T)[:, None], e_idx].set(w)
    gates = gates.astype(t.dtype)

    def expert(acc, xs):
        wg, wu, wd, g = xs
        h = jax.nn.silu(t @ wg) * (t @ wu)
        return acc + g[:, None] * (h @ wd), None

    routed, _ = lax.scan(expert, jnp.zeros_like(t), (w_e_gate, w_e_up, w_e_down, gates.T))
    shared = (jax.nn.silu(t @ w_s_gate) * (t @ w_s_up)) @ w_s_down
    return (routed + shared).reshape(B, S, D)

def setup_inputs(seed: int = 0) -> dict:
    key = jax.random.key(seed)
    ks = jax.random.split(key, 32)
    f32 = jnp.float32
    L = DEPTH

    def nrm(k, shape, s):
        return jax.random.normal(k, shape, f32) * s

    return {
        "x": jax.random.normal(ks[0], (BATCH, SEQ, D_MODEL), f32),
        "w_in": nrm(ks[1], (L, D_MODEL, D_IN), D_MODEL ** -0.5),
        "hg_lb_logits": nrm(ks[2], (DEPTH + 1, HG_HEADS * HG_DK), 0.1),
        "hg_norm_g": 1.0 + nrm(ks[3], (L, HG_DV), 0.02),
        "q_norm_g": 1.0 + nrm(ks[4], (L, Q_RANK), 0.02),
        "w_q_up": nrm(ks[5], (L, Q_RANK, AT_WIDTH), Q_RANK ** -0.5),
        "w_qidx_up": nrm(ks[6], (L, Q_RANK, IDX_HEADS * IDX_DH), Q_RANK ** -0.5),
        "kv_norm_g": 1.0 + nrm(ks[7], (L, KV_RANK), 0.02),
        "w_kv_up": nrm(ks[8], (L, KV_RANK, 2 * AT_WIDTH), KV_RANK ** -0.5),
        "idx_ln_g": 1.0 + nrm(ks[9], (L, IDX_DH), 0.02),
        "idx_ln_b": nrm(ks[10], (L, IDX_DH), 0.02),
        "w_out": nrm(ks[11], (L, D_MIX, D_MODEL), BETA * D_MIX ** -0.5),
        "ln1_g": 1.0 + nrm(ks[12], (L, D_MODEL), 0.02),
        "ln1_b": nrm(ks[13], (L, D_MODEL), 0.02),
        "w_router": nrm(ks[14], (L, D_MODEL, N_EXPERTS), D_MODEL ** -0.5),
        "router_bias": nrm(ks[15], (L, N_EXPERTS), 0.01),
        "w_e_gate": nrm(ks[16], (L, N_EXPERTS, D_MODEL, D_EXPERT), D_MODEL ** -0.5),
        "w_e_up": nrm(ks[17], (L, N_EXPERTS, D_MODEL, D_EXPERT), D_MODEL ** -0.5),
        "w_e_down": nrm(ks[18], (L, N_EXPERTS, D_EXPERT, D_MODEL), BETA * D_EXPERT ** -0.5),
        "w_s_gate": nrm(ks[19], (L, D_MODEL, D_SHARED), D_MODEL ** -0.5),
        "w_s_up": nrm(ks[20], (L, D_MODEL, D_SHARED), D_MODEL ** -0.5),
        "w_s_down": nrm(ks[21], (L, D_SHARED, D_MODEL), BETA * D_SHARED ** -0.5),
        "ln2_g": 1.0 + nrm(ks[22], (L, D_MODEL), 0.02),
        "ln2_b": nrm(ks[23], (L, D_MODEL), 0.02),
    }

def reference(x, w_in, hg_lb_logits, hg_norm_g, q_norm_g, w_q_up, w_qidx_up, kv_norm_g, w_kv_up,
              idx_ln_g, idx_ln_b, w_out, ln1_g, ln1_b, w_router, router_bias, w_e_gate, w_e_up,
              w_e_down, w_s_gate, w_s_up, w_s_down, ln2_g, ln2_b):
    h = x
    lb_all = jnp.cumsum(jax.nn.softmax(hg_lb_logits.astype(jnp.float32), axis=0), axis=0)
    for l in range(DEPTH):
        proj = h @ w_in[l]
        hq, hf, hi, hg, cq, ckv, kidx, widx = jnp.split(proj, IN_SPLITS, axis=-1)
        o_a = hgrn2_mixer(hq, hf, hi, hg, lb_all[l], hg_norm_g[l])
        o_b = dsa_mixer(cq, ckv, kidx, widx, q_norm_g[l], w_q_up[l], w_qidx_up[l], kv_norm_g[l],
                        w_kv_up[l], idx_ln_g[l], idx_ln_b[l])
        mix = jnp.concatenate([o_a.astype(h.dtype), o_b.astype(h.dtype)], axis=-1) @ w_out[l]
        h = layer_norm(ALPHA * h + mix, ln1_g[l], ln1_b[l])
        ffn = moe_ffn(h, w_router[l], router_bias[l], w_e_gate[l], w_e_up[l], w_e_down[l],
                      w_s_gate[l], w_s_up[l], w_s_down[l])
        h = layer_norm(ALPHA * h + ffn, ln2_g[l], ln2_b[l])
    return h


_drawn_inputs = setup_inputs


def setup_inputs(seed=0):
    import zlib

    import numpy as np

    out = dict(_drawn_inputs(seed))
    spreads = {}
    factors = {'hg_lb_logits': 6.32,
     'hg_norm_g': 3.286,
     'kv_norm_g': 3.865,
     'ln2_g': 2.827,
     'ln2_b': 2.91}
    for name, (base, spread) in spreads.items():
        noise = np.random.default_rng([zlib.crc32(name.encode()), seed]).standard_normal(out[name].shape)
        drawn = base * np.exp(spread * noise) if base else spread * noise
        out[name] = __import__('jax').numpy.asarray(drawn.astype(out[name].dtype))
    for name, factor in factors.items():
        out[name] = (out[name] * factor).astype(out[name].dtype)
    return out
```

```python
from contextlib import ExitStack

import concourse.bass as bass
from concourse import mybir

ALU = mybir.AluOpType
ACT = mybir.ActivationFunctionType
AX = mybir.AxisListType
F32 = mybir.dt.float32
I32 = mybir.dt.int32

P = 128
SEQ, DM = 512, 1024
NT = SEQ // P
KD = DM // P
CHUNK = 64
NCH = SEQ // CHUNK
HG, DK, DV = 4, 128, 128
AH, DH = 8, 64
AW = AH * DH
QR, KVR = 256, 128
IH, IDH = 4, 64
TOPK = 128
NE, TK, NG, TG = 64, 8, 8, 4
PER = NE // NG
DE = 256
ROUTED_SCALE = 2.5
ALPHA = 2.0 ** 0.25
LN_EPS, RMS_EPS = 1e-5, 1e-6
CQ0 = 2048
BIG = 16384.0
NEG = 1e30
CAP = 96
MAXC = -(-SEQ // CAP)
RING = 7
SLOTS = 4
GROUPS = NE // SLOTS


def hybrid_block(nc, x, w_in, hg_lb_logits, hg_norm_g, q_norm_g, w_q_up, w_qidx_up, kv_norm_g, w_kv_up,
                 idx_ln_g, idx_ln_b, w_out, ln1_g, ln1_b, w_router, router_bias, w_e_gate, w_e_up,
                 w_e_down, w_s_gate, w_s_up, w_s_down, ln2_g, ln2_b, out, dbg=None):
    h_rows = nc.dram_tensor("h_rows", (SEQ, DM), F32).ap()
    y_rows = nc.dram_tensor("y_rows", (SEQ * TK, DM), F32).ap()

    with ExitStack() as ctx:
        def sb(name, shape, dt=F32):
            return ctx.enter_context(nc.sbuf_tensor(name, shape, dt))

        def sem(name):
            return ctx.enter_context(nc.semaphore(name))

        WORDS = 50432
        arena = sb("arena", [P, WORDS])

        def at(start, *shape):
            n = 1
            for d in shape:
                n *= d
            v = arena[:, start:start + n]
            if len(shape) == 1:
                return v
            names = " ".join(f"d{i}" for i in range(len(shape)))
            return v.rearrange(f"p ({names}) -> p {names}", **{f"d{i}": s for i, s in enumerate(shape[:-1])})

        EW = KD * 2 * DE + 2 * DM
        SLOT_AT = [0, EW, 2 * EW, 22528]
        w_gu = [at(s, 2, KD, DE) for s in SLOT_AT]
        w_dn = [at(s + KD * 2 * DE, 2, DM) for s in SLOT_AT]
        w_lat = at(6144, KD, 516)
        w_blk = [at(10272, KD, 256), at(12320, KD, 256)]
        w_o = at(6144, KD, DM)
        lf = at(14368, HG, SEQ)
        o_hg = lf
        wq_up = at(16416, 2, 512)
        wqi_up = at(17440, 2, 256)
        x_nat = at(18432, NT, DM)
        xT = at(22528, KD, SEQ)
        oT = xT
        qT = at(26624, 4, SEQ)
        kT = at(28672, 4, SEQ)
        v_at = at(30720, NT, AW)
        MASK_AT = [32768, 32896, 33152, 33536]
        sel_mask = [at(MASK_AT[t], (t + 1) * P) for t in range(NT)]
        kf = at(34048, HG, SEQ)
        sT = kf
        enb = at(36096, HG, SEQ)
        mix_a = enb
        eb = at(38144, HG, SEQ)
        kdN = eb
        qs = at(40192, HG, SEQ)
        v_hg = at(42240, NT, HG * DV)
        gate = at(44288, NT, HG * DV)
        wkv_up = at(46336, 2 * AW)
        cqT = at(47360, 2, SEQ)
        ckT = at(48384, SEQ)
        kxT = at(48896, SEQ)
        qiT = at(49408, 2, SEQ)
        states = at(46336, 2, NCH, DV)
        sq = at(18432, 3, SEQ)
        rt = at(18432 + 1536, 3, SEQ)
        sqk = at(18432 + 3072, SEQ)
        score = at(18432, SEQ)
        work = at(18432 + 512, SEQ)
        m_eq = at(18432 + 1024, SEQ)
        m_cum = at(18432 + 1536, SEQ)
        relu_t = at(18432 + 2048, 2, SEQ)
        at_bias = at(18432, 2, SEQ)
        at_s = at(18432 + 1024, 2, SEQ)
        at_p = at(18432 + 2048, 2, SEQ)
        at_pT = at(18432 + 3072, 2, SEQ)
        acc = at(34048, NT, DM)
        ln_g = at(18432, DM)
        ln_b = at(18432 + 1024, DM)
        hT = at(38144, KD, SEQ)
        ws_gu = at(42240, 2, KD, DE)
        ws_dn = at(46336, 2, DM)
        silu_g = at(48384, 2, DE)
        h_e = at(48896, 2, DE)
        heT = at(49408, 2, DE)
        heT_x = at(49408, 2, 2 * CAP)
        R = [at(18432 + 2048 + 256 * i, NT, NE) for i in range(8)]
        w_rt = at(33536, KD, NE)
        pos_x = at(28672, MAXC * NE, NT)
        meta = at(28672 + MAXC * NE * NT, NE, NT, 3)
        place = at(32768, 2, NT, CAP)
        xg = at(38144, SLOTS, DM)
        xgT = at(42240, 2, KD * CAP)
        y_sb = at(44288, SLOTS, DM)
        y_sum = at(38144, 2, DM)
        y_in = at(0, 2, TK, DM)

        ident = sb("ident", [P, P])
        ones = sb("ones", [P, P])
        lower = sb("lower", [P, P])
        dist = sb("dist", [P, SEQ])
        keep = sb("keep", [P, SEQ])
        slot_id = sb("slot_id", [P, P])
        tok_id = sb("tok_id", [P, NT])
        norm_row = sb("norm_row", [P, DV])
        bias_row = sb("bias_row", [P, NE])
        before = sb("before", [P, NG, NG])
        lbl = sb("lbl", [P, 2, HG])
        lb = sb("lb", [P, HG])
        one_lb = sb("one_lb", [P, HG])
        gq = sb("gq", [P, 2])
        gkv = sb("gkv", [P, 1])
        gk = sb("gk", [P, 1])
        bk = sb("bk", [P, 1])
        w_i = sb("w_i", [P, NT, IH])
        top8 = sb("top8", [P, 8])
        cnt = sb("cnt", [P, 2])
        dec = sb("dec", [P, HG, NCH])
        ss_o = sb("ss_o", [P, HG, NT])
        r_o = sb("r_o", [P, HG, NT])
        nmax = sb("nmax", [P, AH * NT])
        rsum = sb("rsum", [P, AH * NT])
        rinv = sb("rinv", [P, AH * NT])
        stats = sb("stats", [P, 2, 6])
        mv = sb("mv", [P, NT, 2])
        rs = sb("rs", [P, NT])
        eps_t = sb("eps_t", [P, 3])
        g1 = sb("g1", [P, NT * NG])
        g2 = sb("g2", [P, NT * NG])
        g3 = sb("g3", [P, NT * NG])
        gr = sb("gr", [P, NT, NG, NG])
        gr2 = at(32768, NT, NG, NG)
        t8 = sb("t8", [P, NT, 8])
        s4 = sb("s4", [P, NT])
        s5 = sb("s5", [P, NT])
        n_max = sb("n_max", [P, MAXC])
        n_int = sb("n_int", [P, 1], I32)
        idx_g = sb("idx_g", [P, SLOTS], I32)
        idx_s = sb("idx_s", [P, SLOTS], I32)
        slot_v = sb("slot_v", [P, SLOTS, 2])

        ps = ctx.enter_context(nc.psum_tensor("ps", [P, 8, 512], F32))

        names = """ld_x0 ld_x1 ld_x2 ld_x3 ld_lat ld_blk0 ld_blk1 ld_small ld_up ld_wo ld_xr ld_ln ld_ln2 ld_rt
            ld_sgu ld_sdn consts const_step units xT_a xT_v lat_a kx_a wi_v sig_a f_v lnf_a sqrt_a norm_v
            xc_v sqk_a kn_v qidx_a relu_a idxs_v up_a mask_v exp_a dec_p qs_a vh_a gate_a gate_p bsum_v
            kd_a sc_a sc_p st_v o_a sq_a ro_v rsq_a oa_v oT_a biasd_v prob_a norm2_v pT_a pv_a res_v
            lnv_v lns_a lnn_v lng_p st_h hT_a hT_v rl_a ro_done sh_si sh_h sh_t sh_y pos_m nch_ready
            link_v link_a link_p lb_v lb_a place_v idxm idx_v turn_p xg_clear ln2n_v ln2v_v sum_v xg_ld xt_m ht_a ro_sel xt_e gu_m si_a h_v ht_m ht_v dn_m
            y_a y_v y_st ln2s_a fin_v fin_p out_st y_ld0 y_ld1 dbg_s""".split()
        S = {n: sem(n) for n in names}
        W_GU = [sem(f"ld_gu{s}") for s in range(SLOTS)]
        W_DN = [sem(f"ld_dn{s}") for s in range(SLOTS)]
        X_GA = [sem(f"gathered{s}") for s in range(SLOTS)]
        Y_ST = [sem(f"scattered{s}") for s in range(SLOTS)]

        units = []

        def unit(name, read_by, count):
            units.append((name, read_by, count))

        for t in range(NT):
            unit(f"xt{t}0", "xT_v", t + 1)
            unit(f"xt{t}1", "xT_a", t + 1)
        for n, name in enumerate(("cq0", "cq1", "ckv")):
            unit(name, "lat_a", n + 1)
        unit("kidx", "kx_a", 1)
        unit("widx", "wi_v", 1)
        unit("hf0", "sig_a", 1)
        unit("ss_cq", "sqrt_a", 1)
        unit("ss_ckv", "sqrt_a", 2)
        unit("mean_k", "xc_v", 1)
        unit("hf1", "sig_a", 2)
        unit("var_k", "sqrt_a", 3)
        unit("hf2", "sig_a", 3)
        unit("qidx0", "qidx_a", 1)
        unit("hf3", "sig_a", 4)
        unit("qidx1", "qidx_a", 2)

        def logits(t):
            for i in range(IH):
                unit(f"lg{t}{i}", "relu_a", IH * (t - 1) + i + 1)

        logits(1)
        for m in range(4):
            unit(f"qu{m}", "up_a", m + 1)
        for m in range(4):
            unit(f"ku{m}", "up_a", 4 + m + 1)
        logits(2)
        for t in range(NT):
            unit(f"vu{t}", "up_a", 8 + t + 1)
        for h in range(HG):
            unit(f"hq{h}", "qs_a", h + 1)
        logits(3)
        for b in range(2):
            for t in range(NT):
                unit(f"hi{b}{t}", "vh_a", NT * b + t + 1)
        for b in range(2):
            for t in range(NT):
                unit(f"hg{b}{t}", "gate_a", NT * b + t + 1)
        for h in range(HG + 1):
            if h < HG:
                unit(f"kd{h}", "kd_a", h + 1)
                unit(f"sc{h}", "sc_a", h + 1)
                unit(f"dsa{h}", "st_v", 7 * h + 7)
                unit(f"dsb{h}", "st_v", 7 * h + 6)
            if h:
                unit(f"o{h - 1}", "o_a", h)
        pairs = [(t, h) for t in range(NT) for h in range(AH)]
        for i in range(len(pairs) + 3):
            if i < len(pairs):
                unit("S%d%d" % pairs[i], "biasd_v", 2 * i + 2)
                t, h = pairs[i]
                if t and h in (3, 6):
                    half = h // 6
                    unit(f"out{t - 1}{half}", "res_v", 2 * (t - 1) + half + 1)
                if t == 0 and h in (2, 3, 4, 5):
                    unit(f"oaT{h - 2}", "oT_a", h - 1)
            if 0 <= i - 2 < len(pairs):
                unit("PT%d%d" % pairs[i - 2], "pT_a", i - 1)
            if 0 <= i - 3 < len(pairs) and pairs[i - 3][1] % 2:
                t, h = pairs[i - 3]
                unit(f"PV{t}{h // 2}", "pv_a", (i - 3) // 2 + 1)
        for half in range(2):
            unit(f"out{NT - 1}{half}", "res_v", 2 * (NT - 1) + half + 1)

        def normed_units(t):
            unit(f"hT{t}0", "hT_v", t + 1)
            unit(f"hT{t}1", "hT_a", t + 1)
            unit(f"rl{t}", "rl_a", t + 1)

        for t in range(NT - 1):
            normed_units(t)
        unit("sg0", "sh_h", 1)
        normed_units(NT - 1)
        for t in range(1, NT):
            unit(f"sg{t}", "sh_h", t + 1)
        for t in range(NT):
            unit(f"st{t}", "sh_t", t + 1)
            unit(f"sd{t}0", "sh_y", 2 * t + 1)
            unit(f"sd{t}1", "sh_y", 2 * t + 2)
        number = {u[0]: n for n, u in enumerate(units)}

        def made(name):
            return number[name] + 1

        def bank(name):
            return ps[:, number[name] % RING, :]

        def pe_unit(pe, name):
            n = number[name]
            if n >= RING:
                _, read_by, count = units[n - RING]
                pe.wait_ge(S[read_by], count)
            return ps[:, n % RING, :]

        def i2(u):
            return u % 2

        def stored_before(u, n, first):
            if first or (u == 0 and isinstance(n, int)):
                return None
            return n * 16 if u else (n - 1) * 16


        def linker(eng, which):
            n = [0]

            def link(ins):
                n[0] += 1
                ins.then_inc(S[which], 1)
                eng.wait_ge(S[which], n[0])
            return link

        block = ctx.enter_context(nc.Block())
        x2 = x.rearrange("b s d -> (b s) d")
        out2 = out.rearrange("b s d -> (b s) d")
        w_in_v = w_in[0].rearrange("(p k) c -> p k c", k=KD)
        gate_w = w_e_gate[0]
        up_w = w_e_up[0]
        down_w = w_e_down[0]

        @block.sync
        def _(sp):
            for t in range(NT):
                sp.dma_start(x_nat[:, t, :], x2[t * P:(t + 1) * P, :]).then_inc(S[f"ld_x{t}"], 16)
            sp.dma_start(w_lat[:, :, 0:448], w_in_v[:, :, CQ0:CQ0 + 448]).then_inc(S["ld_lat"], 16)
            sp.dma_start(w_lat[:, :, 448:512], w_in_v[:, :, CQ0 + 384:CQ0 + 448]).then_inc(S["ld_lat"], 16)
            sp.dma_start(w_lat[:, :, 512:516], w_in_v[:, :, CQ0 + 448:CQ0 + 452]).then_inc(S["ld_lat"], 16)
            cols = [512, 768, 0, 256, 1024, 1280, 1536, 1792]
            last_use = ["hf1", "hf3", "hq1", "hq3", "hi03", "hi13", "hg03", "hg13"]
            for j, c in enumerate(cols):
                if j >= 2:
                    sp.wait_ge(S["units"], made(last_use[j - 2]))
                sp.dma_start(w_blk[j % 2][:, :, :], w_in_v[:, :, c:c + 256]).then_inc(S[f"ld_blk{j % 2}"], 16)
                if j == 1:
                    sp.dma_start(wqi_up, w_qidx_up[0].rearrange("(m p) c -> p m c", p=P)).then_inc(S["ld_up"], 16)
                    sp.dma_start(wq_up, w_q_up[0].rearrange("(m p) c -> p m c", p=P)).then_inc(S["ld_up"], 16)
                    sp.dma_start(wkv_up, w_kv_up[0]).then_inc(S["ld_up"], 16)
                if j == 3:
                    sp.dma_start(w_gu[0][:, 0], gate_w[0].rearrange("(p k) f -> p k f", k=KD)).then_inc(W_GU[0], 16)
                    sp.dma_start(w_gu[0][:, 1], up_w[0].rearrange("(p k) f -> p k f", k=KD)).then_inc(W_GU[0], 16)
                    sp.dma_start(w_dn[0], down_w[0].rearrange("(p k) n -> p k n", k=2)).then_inc(W_DN[0], 16)
            sp.wait_ge(S["units"], made("hg13"))
            sp.dma_start(w_o, w_out[0].rearrange("(m p) n -> p m n", p=P)).then_inc(S["ld_wo"], 16)
            sp.wait_ge(S["oT_a"], HG)
            sp.dma_start(acc, x2.rearrange("(t p) d -> p t d", p=P)).then_inc(S["ld_xr"], 16)
            sp.wait_ge(S["o_a"], HG)
            sp.wait_ge(S["oT_a"], HG)
            sp.dma_start(ws_gu[:, 0], w_s_gate[0].rearrange("(p k) f -> p k f", k=KD)).then_inc(S["ld_sgu"], 16)
            sp.dma_start(ws_gu[:, 1], w_s_up[0].rearrange("(p k) f -> p k f", k=KD)).then_inc(S["ld_sgu"], 16)
            sp.dma_start(ws_dn, w_s_down[0].rearrange("(p k) n -> p k n", k=2)).then_inc(S["ld_sdn"], 16)
            sp.wait_ge(S["pv_a"], len(pairs) // 2)
            sp.dma_start(ln_g, ln1_g[0:1, :].broadcast_to([P, DM])).then_inc(S["ld_ln"], 16)
            sp.dma_start(ln_b, ln1_b[0:1, :].broadcast_to([P, DM])).then_inc(S["ld_ln"], 16)
            sp.dma_start(w_rt, w_router[0].rearrange("(p k) e -> p k e", k=KD)).then_inc(S["ld_rt"], 16)
            sp.wait_ge(S["units"], made(f"out{NT - 1}1"))

            def load_expert(e, s):
                sp.dma_start(w_gu[s][:, 0], gate_w[bass.ds(e, 1)].rearrange("e (p k) f -> (e p) k f", k=KD)).then_inc(W_GU[s], 16)
                sp.dma_start(w_gu[s][:, 1], up_w[bass.ds(e, 1)].rearrange("e (p k) f -> (e p) k f", k=KD)).then_inc(W_GU[s], 16)
                sp.dma_start(w_dn[s], down_w[bass.ds(e, 1)].rearrange("e (p k) n -> (e p) k n", k=2)).then_inc(W_DN[s], 16)

            for s in range(1, SLOTS):
                load_expert(s, s)
            for t in range(NT):
                sp.wait_ge(S["lng_p"], 2 * t + 2)
                sp.dma_start(h_rows[t * P:(t + 1) * P, :], acc[:, t, :]).then_inc(S["st_h"], 16)
            sp.wait_ge(S["lng_p"], 2 * NT)
            sp.dma_start(ln_g, ln2_g[0:1, :].broadcast_to([P, DM])).then_inc(S["ld_ln2"], 16)
            sp.dma_start(ln_b, ln2_b[0:1, :].broadcast_to([P, DM])).then_inc(S["ld_ln2"], 16)
            sp.wait_ge(S["nch_ready"], 1)
            n_mid = sp.value_load(n_int[0:1, 0:1], min_val=GROUPS - 2, max_val=GROUPS * MAXC - 2)
            with sp.Fori(1, n_mid + 2) as g:
                first = sp.snap((g % GROUPS) * SLOTS)
                for s in range(SLOTS):
                    gate_e = gate_w[bass.ds(first + s, 1)].rearrange("e (p k) f -> (e p) k f", k=KD)
                    up_e = up_w[bass.ds(first + s, 1)].rearrange("e (p k) f -> (e p) k f", k=KD)
                    down_e = down_w[bass.ds(first + s, 1)].rearrange("e (p k) n -> (e p) k n", k=2)
                    used = sp.snap(g * SLOTS + (s + 1 - SLOTS))
                    sp.wait_ge(S["gu_m"], used)
                    sp.dma_start(w_gu[s][:, 0], gate_e).then_inc(W_GU[s], 16)
                    sp.dma_start(w_gu[s][:, 1], up_e).then_inc(W_GU[s], 16)
                    sp.wait_ge(S["dn_m"], used)
                    sp.dma_start(w_dn[s], down_e).then_inc(W_DN[s], 16)
            items = sp.snap(n_mid * SLOTS + 2 * SLOTS)
            stored = sp.snap(n_mid * 16 + 32)
            sp.wait_ge(S["dn_m"], items)
            for s in range(SLOTS):
                sp.wait_ge(Y_ST[s], stored)
            y_v8 = y_rows.rearrange("(t p k) d -> t p k d", p=P, k=TK)
            for t in range(NT):
                if t >= 2:
                    sp.wait_ge(S["fin_v"], t - 1)
                sp.dma_start(y_in[:, t % 2], y_v8[t]).then_inc(S[f"y_ld{t % 2}"], 16)
            for t in range(NT):
                sp.wait_ge(S["fin_p"], 2 * t + 2)
                sp.dma_start(out2[t * P:(t + 1) * P, :], acc[:, t]).then_inc(S["out_st"], 16)
            sp.wait_ge(S["out_st"], 16 * NT)
            if dbg is not None:
                sp.dma_start(dbg[0:SEQ], h_rows).then_inc(S["dbg_s"], 16)
                sp.wait_ge(S["dbg_s"], 16)

        @block.gpsimd
        def _(pool):
            link = linker(pool, "link_p")
            g = nc.gpsimd
            small = [
                (lbl[:], hg_lb_logits.rearrange("r (h p) -> p r h", p=P)),
                (gq[:], q_norm_g[0].rearrange("(m p) -> p m", p=P)),
                (gkv[:], kv_norm_g[0].rearrange("(p o) -> p o", o=1)),
                (gk[0:IDH, :], idx_ln_g[0].rearrange("(p o) -> p o", o=1)),
                (gk[IDH:P, :], idx_ln_g[0].rearrange("(p o) -> p o", o=1)),
                (bk[0:IDH, :], idx_ln_b[0].rearrange("(p o) -> p o", o=1)),
                (bk[IDH:P, :], idx_ln_b[0].rearrange("(p o) -> p o", o=1)),
                (norm_row[:], hg_norm_g[0:1, :].broadcast_to([P, DV])),
                (bias_row[:], router_bias[0:1, :].broadcast_to([P, NE])),
            ]
            g.memset(ident[:], 0.0).then_inc(S["const_step"], 1)
            g.memset(ones[:], 1.0)
            g.memset(keep[:], 1.0)
            g.memset(lower[:], 1.0)
            g.memset(before[:], 1.0)
            g.memset(eps_t[:, 0:1], RMS_EPS)
            g.memset(eps_t[:, 1:2], LN_EPS).then_inc(S["const_step"], 1)
            pool.wait_ge(S["const_step"], 2)
            g.affine_select(out=ident[:], in_=ident[:], compare_op=ALU.not_equal, fill=1.0, base=0,
                            pattern=[[-1, P]], channel_multiplier=1).then_inc(S["consts"], 1)
            for dst, src in small:
                pool.dma_start(dst, src, allow_slow_non_contiguous=True).then_inc(S["ld_small"], 16)
            g.affine_select(out=lower[:], in_=lower[:], compare_op=ALU.is_gt, fill=0.0, base=0,
                            pattern=[[1, P]], channel_multiplier=-1)
            g.affine_select(out=before[:], in_=before[:], compare_op=ALU.is_gt, fill=0.0, base=0,
                            pattern=[[1, NG], [-1, NG]], channel_multiplier=0)
            g.iota(dist[:], pattern=[[-1, SEQ]], base=SEQ - P, channel_multiplier=1,
                   allow_small_or_imprecise_dtypes=True)
            g.iota(slot_id[:], pattern=[[1, P]], base=0, channel_multiplier=0, allow_small_or_imprecise_dtypes=True)
            g.iota(tok_id[:], pattern=[[P, NT]], base=0, channel_multiplier=1, allow_small_or_imprecise_dtypes=True)
            g.memset(keep[:].rearrange("p (c s) -> p c s", s=CHUNK)[:, :, 0:1], 0.0).then_inc(S["consts"], 1)
            for h in range(HG):
                pool.wait_ge(S["exp_a"], 4 * h + 4)
                g.tensor_tensor(enb[:, h], kf[:, h], enb[:, h], ALU.mult)
                g.tensor_tensor(lf[:, h], kf[:, h], lf[:, h], ALU.mult)
                pool.wait_ge(S["qs_a"], h + 1)
                g.tensor_tensor(qs[:, h], qs[:, h], eb[:, h], ALU.mult).then_inc(S["dec_p"], 1)
            for n in range(2 * NT):
                b, t = n // NT, n % NT
                pool.wait_ge(S["gate_a"], n + 1)
                gv = gate[:, t, b * 256:(b + 1) * 256].rearrange("p (h v) -> p h v", v=DV)
                g.tensor_tensor(gv, gv, norm_row[:].unsqueeze(1).broadcast_to([P, 2, DV]), ALU.mult)\
                    .then_inc(S["gate_p"], 1)
            for h in range(HG):
                pool.wait_ge(S["sc_a"], h + 1)
                sv = sT[:, h].rearrange("p (t c) -> p t c", c=P)
                link(g.affine_select(out=sv, in_=sv, compare_op=ALU.is_ge, fill=0.0, base=0,
                                     pattern=[[0, NT], [1, P]], channel_multiplier=-1))
                g.memset(sv[0:CHUNK, :, CHUNK:P], 0.0).then_inc(S["sc_p"], 1)
            pool.wait_ge(S["ld_ln"], 32)
            for t in range(NT):
                pool.wait_ge(S["lnn_v"], t + 1)
                g.tensor_tensor(acc[:, t], acc[:, t], ln_g, ALU.mult).then_inc(S["lng_p"], 1)
                pool.wait_ge(S["lng_p"], 2 * t + 1)
                g.tensor_tensor(acc[:, t], acc[:, t], ln_b, ALU.add).then_inc(S["lng_p"], 1)
            pool.wait_ge(S["units"], made(f"sg{NT - 1}"))
            g.memset(xg[:], 0.0).then_inc(S["xg_clear"], 1)
            pool.wait_ge(S["xg_clear"], 1)
            pool.wait_ge(S["st_h"], 16 * NT)
            pool.wait_ge(S["nch_ready"], 1)
            n_mid = pool.value_load(n_int[0:1, 0:1], min_val=GROUPS - 2, max_val=GROUPS * MAXC - 2)

            last_token = pool.to_reg(SEQ - 1)
            last_row = pool.to_reg(SEQ * TK - 1)

            def gather(i, u):
                pool.wait_ge(S["st_h"], 16 * NT)
                pool.wait_ge(S["idx_v"], i + 1)
                if not isinstance(i, int) or i >= SLOTS:
                    pool.wait_ge(S["xt_m"], i + (1 - SLOTS))
                pool.sem_inc(S["turn_p"], 1)
                pool.indirect_dma_start(out=xg[0:CAP, u, :], out_offset=None, in_=h_rows,
                                        in_offset=bass.IndirectOffsetOnAxis(ap=idx_g[0:CAP, u:u + 1], axis=0),
                                        bounds_check=last_token, oob_is_err=False).then_inc(X_GA[u], 16)

            def scatter(i, u):
                pool.wait_ge(S["y_a"], i + 1)
                pool.wait_ge(S["y_v"], i + 1)
                pool.sem_inc(S["turn_p"], 1)
                pool.indirect_dma_start(out=y_rows, out_offset=bass.IndirectOffsetOnAxis(ap=idx_s[0:CAP, u:u + 1], axis=0),
                                        in_=y_sb[0:CAP, u, :], in_offset=None,
                                        bounds_check=last_row, oob_is_err=False).then_inc(Y_ST[u], 16)

            def group(i0, first=False, last=False):
                for u in range(SLOTS):
                    if not (last and u >= 1):
                        gather(i0 + (u + 3), (u + 3) % SLOTS)
                    if not (first and u == 0):
                        scatter(i0 + (u - 1), (u + 3) % SLOTS)

            gather(0, 0)
            gather(1, 1)
            gather(2, 2)
            group(0, first=True)
            with pool.Fori(1, n_mid + 1) as n:
                group(pool.snap(n * SLOTS))
            i0 = pool.snap(n_mid * SLOTS + SLOTS)
            group(i0, last=True)
            scatter(i0 + 3, 3)
            pool.wait_ge(S["ld_ln2"], 32)
            for t in range(NT):
                pool.wait_ge(S["ln2n_v"], t + 1)
                g.tensor_tensor(acc[:, t], acc[:, t], ln_g, ALU.mult).then_inc(S["fin_p"], 1)
                pool.wait_ge(S["fin_p"], 2 * t + 1)
                g.tensor_tensor(acc[:, t], acc[:, t], ln_b, ALU.add).then_inc(S["fin_p"], 1)

        @block.scalar
        def _(act):
            a = nc.scalar

            def copy(o, i):
                return a.activation(o, i, ACT.Copy)

            for t in range(NT):
                act.wait_ge(S["units"], made(f"xt{t}1"))
                copy(xT[:, 4:8, t * P:(t + 1) * P], bank(f"xt{t}1").rearrange("p (k c) -> p k c", c=P)).then_inc(S["xT_a"], 1)
            for n, name in enumerate(("cq0", "cq1", "ckv")):
                act.wait_ge(S["units"], made(name))
                copy(cqT[:, n] if n < 2 else ckT, bank(name))
                a.activation(sq[:, n], bank(name), ACT.Square).then_inc(S["lat_a"], 1)
            act.wait_ge(S["units"], made("kidx"))
            copy(kxT, bank("kidx")).then_inc(S["kx_a"], 1)
            act.wait_ge(S["lb_v"], 1)
            a.activation(lbl[:], lbl[:], ACT.Exp).then_inc(S["lb_a"], 1)
            act.wait_ge(S["units"], made("hf0"))
            a.activation(lf[:, 0], bank("hf0"), ACT.Sigmoid).then_inc(S["sig_a"], 1)
            act.wait_ge(S["consts"], 2)
            a.activation(dist[:], dist[:], ACT.Abs)
            act.wait_ge(S["units"], made("ss_cq"))
            a.activation(rt[:, 0], bank("ss_cq"), ACT.Sqrt, bias=eps_t[:, 0:1], scale=1.0 / QR).then_inc(S["sqrt_a"], 1)
            act.wait_ge(S["units"], made("ss_ckv"))
            a.activation(rt[:, 1], bank("ss_ckv"), ACT.Sqrt, bias=eps_t[:, 0:1], scale=1.0 / KVR).then_inc(S["sqrt_a"], 1)
            act.wait_ge(S["xc_v"], 1)
            a.activation(sqk, kxT, ACT.Square).then_inc(S["sqk_a"], 1)
            act.wait_ge(S["units"], made("var_k"))
            a.activation(rt[:, 2], bank("var_k"), ACT.Sqrt, bias=eps_t[:, 1:2], scale=1.0 / P).then_inc(S["sqrt_a"], 1)
            for h in range(1, HG):
                act.wait_ge(S["units"], made(f"hf{h}"))
                a.activation(lf[:, h], bank(f"hf{h}"), ACT.Sigmoid).then_inc(S["sig_a"], 1)
            for m in range(2):
                act.wait_ge(S["units"], made(f"qidx{m}"))
                copy(qiT[:, m], bank(f"qidx{m}")).then_inc(S["qidx_a"], 1)
            for h in range(HG):
                act.wait_ge(S["f_v"], h + 1)
                a.activation(lf[:, h], lf[:, h], ACT.Ln).then_inc(S["lnf_a"], 1)

            def relus(t):
                for i in range(IH):
                    n = IH * (t - 1) + i
                    act.wait_ge(S["units"], made(f"lg{t}{i}"))
                    if n >= 2:
                        act.wait_ge(S["idxs_v"], n - 1)
                    a.activation(relu_t[:, n % 2, 0:(t + 1) * P], bank(f"lg{t}{i}")[:, 0:(t + 1) * P],
                                 ACT.Relu).then_inc(S["relu_a"], 1)

            relus(1)
            for m in range(4):
                act.wait_ge(S["units"], made(f"qu{m}"))
                a.activation(qT[:, m], bank(f"qu{m}"), ACT.Copy, scale=DH ** -0.5).then_inc(S["up_a"], 1)
            for m in range(4):
                act.wait_ge(S["units"], made(f"ku{m}"))
                copy(kT[:, m], bank(f"ku{m}")).then_inc(S["up_a"], 1)
            for h in range(HG):
                act.wait_ge(S["bsum_v"], 2 * h + 2)
                a.activation(eb[:, h], lf[:, h], ACT.Exp).then_inc(S["exp_a"], 1)
                a.activation(enb[:, h], lf[:, h], ACT.Exp, scale=-1.0).then_inc(S["exp_a"], 1)
                a.activation(dec[:, h], lf[:, h].rearrange("p (c s) -> p c s", s=CHUNK)[:, :, CHUNK - 1], ACT.Exp)\
                    .then_inc(S["exp_a"], 1)
                act.wait_ge(S["exp_a"], 4 * h + 3)
                a.activation(lf[:, h], qs[:, h], ACT.Exp).then_inc(S["exp_a"], 1)
            relus(2)
            for t in range(NT):
                act.wait_ge(S["units"], made(f"vu{t}"))
                copy(v_at[:, t], bank(f"vu{t}")).then_inc(S["up_a"], 1)
            for h in range(HG):
                act.wait_ge(S["units"], made(f"hq{h}"))
                a.activation(qs[:, h], bank(f"hq{h}"), ACT.Silu).then_inc(S["qs_a"], 1)
            relus(3)
            for b in range(2):
                for t in range(NT):
                    act.wait_ge(S["units"], made(f"hi{b}{t}"))
                    copy(v_hg[:, t, b * 256:(b + 1) * 256], bank(f"hi{b}{t}")[:, 0:256]).then_inc(S["vh_a"], 1)
            for b in range(2):
                for t in range(NT):
                    act.wait_ge(S["units"], made(f"hg{b}{t}"))
                    a.activation(gate[:, t, b * 256:(b + 1) * 256], bank(f"hg{b}{t}")[:, 0:256], ACT.Silu)\
                        .then_inc(S["gate_a"], 1)
            for h in range(HG + 1):
                if h < HG:
                    act.wait_ge(S["dec_p"], HG)
                    act.wait_ge(S["units"], made(f"kd{h}"))
                    copy(kdN[:, h], bank(f"kd{h}")).then_inc(S["kd_a"], 1)
                    act.wait_ge(S["units"], made(f"sc{h}"))
                    copy(sT[:, h], bank(f"sc{h}")).then_inc(S["sc_a"], 1)
                if h:
                    act.wait_ge(S["units"], made(f"o{h - 1}"))
                    copy(o_hg[:, h - 1], bank(f"o{h - 1}"))
                    a.activation(qs[:, h - 1], bank(f"o{h - 1}"), ACT.Square).then_inc(S["o_a"], 1)
            act.wait_ge(S["sq_a"], HG)
            a.activation(r_o[:], ss_o[:], ACT.Sqrt, bias=eps_t[:, 0:1], scale=1.0 / DV).then_inc(S["rsq_a"], 1)

            def probs(i):
                t, h = pairs[i]
                n = (t + 1) * P
                act.wait_ge(S["biasd_v"], 2 * i + 2)
                if i >= 2:
                    act.wait_ge(S["units"], made("PT%d%d" % pairs[i - 2]))
                a.activation(at_p[:, i % 2, 0:n], at_s[:, i % 2, 0:n], ACT.Exp, bias=nmax[:, i:i + 1],
                             accum_out=rsum[:, i:i + 1]).then_inc(S["prob_a"], 1)

            def probs_t(i):
                t, h = pairs[i]
                n = (t + 1) * P
                act.wait_ge(S["units"], made("PT%d%d" % (t, h)))
                if i >= 2:
                    tt, hh = pairs[i - 2]
                    act.wait_ge(S["units"], made(f"PV{tt}{hh // 2}"))
                copy(at_pT[:, i % 2, 0:n], bank("PT%d%d" % (t, h))[:, 0:n]).then_inc(S["pT_a"], 1)

            def heads_out(i):
                t, h = pairs[i]
                name = f"PV{t}{h // 2}"
                act.wait_ge(S["units"], made(name))
                copy(oT[:, 4 + h // 2, t * P:(t + 1) * P], bank(name)[:, 0:P]).then_inc(S["pv_a"], 1)

            for i in range(len(pairs) + 3):
                if i < len(pairs):
                    probs(i)
                    t, h = pairs[i]
                    if t == 0 and h in (2, 3, 4, 5):
                        act.wait_ge(S["units"], made(f"oaT{h - 2}"))
                        copy(oT[:, h - 2], bank(f"oaT{h - 2}")).then_inc(S["oT_a"], 1)
                if 0 <= i - 2 < len(pairs):
                    probs_t(i - 2)
                if 0 <= i - 3 < len(pairs) and pairs[i - 3][1] % 2:
                    heads_out(i - 3)

            def rstd(ts):
                for t in ts:
                    act.wait_ge(S["lnv_v"], t + 1)
                    a.activation(rs[:, t:t + 1], mv[:, t, 1:2], ACT.Sqrt, bias=eps_t[:, 1:2]).then_inc(S["lns_a"], 1)

            def normed_rows(ts):
                for t in ts:
                    act.wait_ge(S["units"], made(f"hT{t}1"))
                    copy(hT[:, 4:8, t * P:(t + 1) * P], bank(f"hT{t}1").rearrange("p (k c) -> p k c", c=P))\
                        .then_inc(S["hT_a"], 1)
                for t in ts:
                    act.wait_ge(S["units"], made(f"rl{t}"))
                    a.activation(R[0][:, t], bank(f"rl{t}")[:, 0:NE], ACT.Sigmoid).then_inc(S["rl_a"], 1)

            def shared_silu(t):
                act.wait_ge(S["units"], made(f"sg{t}"))
                if t >= 2:
                    act.wait_ge(S["sh_h"], t - 1)
                a.activation(silu_g[:, t % 2], bank(f"sg{t}")[:, 0:DE], ACT.Silu).then_inc(S["sh_si"], 1)

            def shared_t(t):
                act.wait_ge(S["units"], made(f"st{t}"))
                if t >= 2:
                    act.wait_ge(S["units"], made(f"sd{t - 2}1"))
                copy(heT[:, t % 2], bank(f"st{t}")[:, 0:DE]).then_inc(S["sh_t"], 1)

            rstd(range(NT))
            normed_rows(range(NT - 1))
            normed_rows([NT - 1])
            for t in range(2):
                shared_silu(t)
            for t in range(NT):
                shared_t(t)
                if t + 2 < NT:
                    shared_silu(t + 2)

            act.wait_ge(S["nch_ready"], 1)
            n_mid = act.value_load(n_int[0:1, 0:1], min_val=GROUPS - 2, max_val=GROUPS * MAXC - 2)

            def rows_t(i, u, early):
                act.wait_ge(S["xt_m"], i + 1)
                if not early:
                    act.wait_ge(S["gu_m"], i - 1)
                copy(xgT[:, i2(u)].rearrange("p (b c) -> p b c", b=2), ps[:, 0:2, 0:KD // 2 * CAP]).then_inc(S["xt_e"], 1)

            def hidden_t(i, u, early):
                act.wait_ge(S["ht_m"], i + 1)
                if not early:
                    act.wait_ge(S["dn_m"], i - 1)
                copy(heT_x[:, i2(u)], ps[:, 4, 0:2 * CAP]).then_inc(S["ht_a"], 1)

            def silu(i, u, early):
                act.wait_ge(S["gu_m"], i + 1)
                if not early:
                    act.wait_ge(S["h_v"], i - 1)
                a.activation(silu_g[0:CAP, i2(u)], ps[0:CAP, 2 + i2(u), 0:DE], ACT.Silu).then_inc(S["si_a"], 1)

            def y_half(i, u, stored):
                act.wait_ge(S["dn_m"], i + 1)
                if stored is not None:
                    act.wait_ge(Y_ST[u], stored)
                copy(y_sb[0:CAP, u, 0:512], ps[0:CAP, 5, :]).then_inc(S["y_a"], 1)

            def group(i0, n, first=False, last=False):
                for u in range(SLOTS):
                    if not (last and u == SLOTS - 1):
                        rows_t(i0 + (u + 1), u + 1, first and u < 1)
                    if not (first and u == 0):
                        hidden_t(i0 + (u - 1), u + 3, first and u < 3)
                    silu(i0 + u, u, first and u < 2)
                    if not (first and u == 0):
                        y_half(i0 + (u - 1), (u + 3) % SLOTS, stored_before(u, n, first))

            rows_t(0, 0, True)
            group(0, 0, first=True)
            with act.Fori(1, n_mid + 1) as n:
                group(act.snap(n * SLOTS), n)
            i0 = act.snap(n_mid * SLOTS + SLOTS)
            n_last = act.snap(n_mid + 1)
            group(i0, n_last, last=True)
            hidden_t(i0 + 3, 3, False)
            y_half(i0 + 3, 3, n_last * 16)
            for t in range(NT):
                act.wait_ge(S["ln2v_v"], t + 1)
                a.activation(rs[:, t:t + 1], mv[:, t, 1:2], ACT.Sqrt, bias=eps_t[:, 1:2]).then_inc(S["ln2s_a"], 1)

        @block.vector
        def _(dve):
            v = nc.vector
            link = linker(dve, "link_v")
            for t in range(NT):
                dve.wait_ge(S["units"], made(f"xt{t}0"))
                v.tensor_copy(xT[:, 0:4, t * P:(t + 1) * P], bank(f"xt{t}0").rearrange("p (k c) -> p k c", c=P))\
                    .then_inc(S["xT_v"], 1)
            dve.wait_ge(S["ld_small"], 144)
            link(v.tensor_tensor(lb[:], lbl[:, 0], lbl[:, 1], ALU.max))
            v.tensor_tensor(lbl[:], lbl[:], lb[:].unsqueeze(1).broadcast_to([P, 2, HG]), ALU.subtract)\
                .then_inc(S["lb_v"], 1)
            dve.wait_ge(S["lb_a"], 1)
            link(v.tensor_tensor(one_lb[:], lbl[:, 0], lbl[:, 1], ALU.add))
            link(v.reciprocal(one_lb[:], one_lb[:]))
            link(v.tensor_tensor(lb[:], lbl[:, 0], one_lb[:], ALU.mult))
            link(v.tensor_scalar(one_lb[:], lb[:], -1.0, 1.0, ALU.mult, ALU.add))
            dve.wait_ge(S["consts"], 2)
            dve.wait_ge(S["units"], made("widx"))
            v.tensor_scalar(w_i[:], bank("widx")[:, 0:NT * IH].rearrange("p (t i) -> p t i", i=IH),
                            IH ** -0.5, IDH ** -0.5, ALU.mult, ALU.mult).then_inc(S["wi_v"], 1)
            dve.wait_ge(S["units"], made("mean_k"))
            v.scalar_tensor_tensor(kxT, bank("mean_k"), -1.0 / P, kxT, ALU.mult, ALU.add).then_inc(S["xc_v"], 1)
            dve.wait_ge(S["sqrt_a"], 2)
            link(v.reciprocal(rt[:, 0:2], rt[:, 0:2]))
            for m in range(2):
                v.scalar_tensor_tensor(cqT[:, m], cqT[:, m], gq[:, m:m + 1], rt[:, 0], ALU.mult, ALU.mult)\
                    .then_inc(S["norm_v"], 1)
            v.scalar_tensor_tensor(ckT, ckT, gkv[:, 0:1], rt[:, 1], ALU.mult, ALU.mult).then_inc(S["norm_v"], 1)
            dve.wait_ge(S["sqrt_a"], 3)
            link(v.reciprocal(rt[:, 2], rt[:, 2]))
            link(v.scalar_tensor_tensor(kxT, kxT, gk[:, 0:1], rt[:, 2], ALU.mult, ALU.mult))
            v.tensor_scalar(kxT, kxT, bk[:, 0:1], None, ALU.add).then_inc(S["kn_v"], 1)
            for h in range(HG):
                dve.wait_ge(S["sig_a"], h + 1)
                link(v.tensor_scalar(lf[:, h], lf[:, h], one_lb[:, h:h + 1], lb[:, h:h + 1], ALU.mult, ALU.add))
                v.tensor_scalar(kf[:, h], lf[:, h], -1.0, 1.0, ALU.mult, ALU.add).then_inc(S["f_v"], 1)
            for h in range(HG):
                dve.wait_ge(S["lnf_a"], h + 1)
                v.tensor_tensor_scan(lf[:, h], keep[:], lf[:, h], 0.0, ALU.mult, ALU.add).then_inc(S["bsum_v"], 1)
                dve.wait_ge(S["bsum_v"], 2 * h + 1)
                bv = lf[:, h].rearrange("p (c s) -> p c s", s=CHUNK)
                v.tensor_tensor(qs[:, h].rearrange("p (c s) -> p c s", s=CHUNK),
                                bv[:, :, CHUNK - 1:CHUNK].broadcast_to([P, NCH, CHUNK]), bv, ALU.subtract)\
                    .then_inc(S["bsum_v"], 1)

            link(v.memset(sel_mask[0][:], 0.0))
            v.memset(sel_mask[0][0:CHUNK, CHUNK:P], -NEG).then_inc(S["mask_v"], 1)
            for t in range(1, NT):
                n = (t + 1) * P
                for i in range(IH):
                    u = IH * (t - 1) + i
                    dve.wait_ge(S["relu_a"], u + 1)
                    if i == 0:
                        ins = v.tensor_scalar(score[:, 0:n], relu_t[:, u % 2, 0:n], w_i[:, t, 0:1], None, ALU.mult)
                    else:
                        ins = v.scalar_tensor_tensor(score[:, 0:n], relu_t[:, u % 2, 0:n], w_i[:, t, i:i + 1],
                                                     score[:, 0:n], ALU.mult, ALU.add)
                    ins.then_inc(S["idxs_v"], 1)
                    dve.wait_ge(S["idxs_v"], u + 1)
                link(v.memset(score[0:CHUNK, n - CHUNK:n], -3e38))
                cur = score
                for r in range(TOPK // 8):
                    link(v.max(top8[:], cur[:, 0:n]))
                    if r < TOPK // 8 - 1:
                        link(v.match_replace(work[:, 0:n], top8[:], cur[:, 0:n], -3.2e38))
                        cur = work
                link(v.tensor_scalar(m_eq[:, 0:n], score[:, 0:n], top8[:, 7:8], None, ALU.is_equal))
                link(v.tensor_tensor_scan(m_cum[:, 0:n], ones[:, 0:1].broadcast_to([P, n]), m_eq[:, 0:n], 0.0, ALU.mult, ALU.add))
                link(v.tensor_scalar(work[:, 0:n], score[:, 0:n], top8[:, 7:8], None, ALU.is_gt, ALU.add,
                                     accum_out=cnt[:, 0:1]))
                link(v.tensor_scalar(cnt[:, 1:2], cnt[:, 0:1], -1.0, float(TOPK), ALU.mult, ALU.add))
                link(v.scalar_tensor_tensor(m_eq[:, 0:n], m_cum[:, 0:n], cnt[:, 1:2], m_eq[:, 0:n], ALU.is_le, ALU.mult))
                link(v.tensor_tensor(work[:, 0:n], work[:, 0:n], m_eq[:, 0:n], ALU.add))
                v.tensor_scalar(sel_mask[t], work[:, 0:n], -1.0, NEG, ALU.add, ALU.mult).then_inc(S["mask_v"], 1)

            for h in range(HG):
                for c in range(NCH - 1):
                    if c == 0:
                        dve.wait_ge(S["units"], made(f"dsb{h}"))
                        if h >= 2:
                            dve.wait_ge(S["units"], made(f"o{h - 2}"))
                    d = bank(f"ds{'ab'[c % 2]}{h}")[:, (c // 2) * DV:(c // 2 + 1) * DV]
                    if c == 0:
                        ins = v.tensor_copy(states[:, h % 2, 1], d)
                    else:
                        ins = v.scalar_tensor_tensor(states[:, h % 2, c + 1], states[:, h % 2, c],
                                                     dec[:, h, c:c + 1], d, ALU.mult, ALU.add)
                    ins.then_inc(S["st_v"], 1)
                    dve.wait_ge(S["st_v"], 7 * h + c + 1)
            for h in range(HG):
                dve.wait_ge(S["o_a"], h + 1)
                v.tensor_reduce(ss_o[:, h], qs[:, h].rearrange("p (t v) -> p t v", v=DV), AX.X, ALU.add)\
                    .then_inc(S["sq_a"], 1)
            dve.wait_ge(S["rsq_a"], 1)
            link(v.reciprocal(r_o[:], r_o[:]))
            dve.wait_ge(S["gate_p"], 2 * NT)
            for h in range(HG):
                ov = o_hg[:, h].rearrange("p (t v) -> p t v", v=DV)
                link(v.tensor_tensor(ov, ov, r_o[:, h].unsqueeze(2).broadcast_to([P, NT, DV]), ALU.mult))
                v.tensor_tensor(mix_a[:, h].rearrange("p (t v) -> p t v", v=DV), ov,
                                gate[:, :, h * DV:(h + 1) * DV], ALU.mult).then_inc(S["oa_v"], 1)

            def scores(i):
                t, h = pairs[i]
                n = (t + 1) * P
                slope = 2.0 ** (-8.0 * (h + 1) / AH)
                link(v.scalar_tensor_tensor(at_bias[:, i % 2, 0:n], dist[:, SEQ - P - t * P:SEQ], -slope,
                                            sel_mask[t], ALU.mult, ALU.add))
                dve.wait_ge(S["units"], made("S%d%d" % (t, h)))
                if i >= 2:
                    dve.wait_ge(S["prob_a"], i - 1)
                v.tensor_tensor(at_s[:, i % 2, 0:n], bank("S%d%d" % (t, h))[:, 0:n], at_bias[:, i % 2, 0:n], ALU.add)\
                    .then_inc(S["biasd_v"], 1)
                dve.wait_ge(S["biasd_v"], 2 * i + 1)
                v.tensor_reduce(nmax[:, i:i + 1], at_s[:, i % 2, 0:n], AX.X, ALU.max, negate=True)\
                    .then_inc(S["biasd_v"], 1)

            def normed(i):
                t, h = pairs[i]
                n = (t + 1) * P
                dve.wait_ge(S["prob_a"], i + 1)
                link(v.reciprocal(rinv[:, i:i + 1], rsum[:, i:i + 1]))
                v.tensor_scalar(at_p[:, i % 2, 0:n], at_p[:, i % 2, 0:n], rinv[:, i:i + 1], None, ALU.mult)\
                    .then_inc(S["norm2_v"], 1)

            def residual(t, half):
                dve.wait_ge(S["units"], made(f"out{t}{half}"))
                dve.wait_ge(S["ld_xr"], 16)
                xv = acc[:, t, half * 512:(half + 1) * 512]
                v.scalar_tensor_tensor(xv, xv, ALPHA, bank(f"out{t}{half}"), ALU.mult, ALU.add)\
                    .then_inc(S["res_v"], 1)

            def row_stats(t):
                dve.wait_ge(S["res_v"], 2 * t + 2)
                link(v.bn_stats(stats[:, 0], acc[:, t, 0:512]))
                link(v.bn_stats(stats[:, 1], acc[:, t, 512:1024]))
                v.bn_aggr(mv[:, t], stats[:]).then_inc(S["lnv_v"], 1)
                dve.wait_ge(S["lnv_v"], t + 1)

            def normalise(ts):
                for t in ts:
                    dve.wait_ge(S["lns_a"], t + 1)
                    link(v.reciprocal(rs[:, t:t + 1], rs[:, t:t + 1]))
                    v.tensor_scalar(acc[:, t], acc[:, t], mv[:, t, 0:1], rs[:, t:t + 1], ALU.subtract, ALU.mult)\
                        .then_inc(S["lnn_v"], 1)

            for i in range(len(pairs) + 1):
                if i < len(pairs):
                    scores(i)
                    t, h = pairs[i]
                    if t and h in (3, 6):
                        residual(t - 1, h // 6)
                if i:
                    normed(i - 1)
            for t in range(NT - 1):
                row_stats(t)
            normalise(range(NT - 1))

            def hidden_rows(ts):
                for t in ts:
                    dve.wait_ge(S["units"], made(f"hT{t}0"))
                    v.tensor_copy(hT[:, 0:4, t * P:(t + 1) * P], bank(f"hT{t}0").rearrange("p (k c) -> p k c", c=P))\
                        .then_inc(S["hT_v"], 1)

            for half in range(2):
                residual(NT - 1, half)
            row_stats(NT - 1)
            normalise([NT - 1])
            hidden_rows(range(NT))

            def shared_h(t):
                dve.wait_ge(S["sh_si"], t + 1)
                if t >= 2:
                    dve.wait_ge(S["units"], made(f"st{t - 2}"))
                v.tensor_tensor(h_e[:, t % 2], silu_g[:, t % 2], bank(f"sg{t}")[:, DE:2 * DE], ALU.mult)\
                    .then_inc(S["sh_h"], 1)

            def shared_y(t):
                for half in range(2):
                    dve.wait_ge(S["units"], made(f"sd{t}{half}"))
                    av = acc[:, t, half * 512:(half + 1) * 512]
                    v.scalar_tensor_tensor(av, av, ALPHA, bank(f"sd{t}{half}"), ALU.mult, ALU.add)\
                        .then_inc(S["sh_y"], 1)

            shared_h(0)
            shared_h(1)
            dve.wait_ge(S["rl_a"], NT)

            def groups_of(r):
                return r.rearrange("p t (g e) -> p (t g) e", e=PER)

            def per_group(r):
                return r[:].unsqueeze(2).broadcast_to([P, NT * NG, PER])

            def per_tile(r, n=NE):
                return r.unsqueeze(2).broadcast_to([P, NT, n])

            def flat(r):
                return r.rearrange("p t e -> p (t e)")

            link(v.tensor_tensor(R[1], R[0], bias_row[:].unsqueeze(1).broadcast_to([P, NT, NE]), ALU.add))
            link(v.tensor_reduce(g1[:], groups_of(R[1]), AX.X, ALU.max))
            link(v.tensor_tensor(groups_of(R[2]), groups_of(R[1]), per_group(g1), ALU.is_equal))
            link(v.tensor_reduce(g2[:], groups_of(R[2]), AX.X, ALU.add))
            link(v.scalar_tensor_tensor(flat(R[3]), flat(R[2]), -NEG, flat(R[1]), ALU.mult, ALU.add))
            link(v.tensor_reduce(g3[:], groups_of(R[3]), AX.X, ALU.max))
            link(v.tensor_scalar(g2[:], g2[:], 2.0, None, ALU.is_ge))
            link(v.tensor_scalar(g2[:], g2[:], -1.0, NEG, ALU.add, ALU.mult))
            link(v.tensor_tensor(g2[:], g2[:], g1[:], ALU.add))
            link(v.tensor_tensor(g3[:], g3[:], g2[:], ALU.max))
            link(v.tensor_tensor(g1[:], g1[:], g3[:], ALU.add))
            gj = g1[:].rearrange("p (t g) -> p t g", g=NG).unsqueeze(2).broadcast_to([P, NT, NG, NG])
            gi = g1[:].rearrange("p (t g) -> p t g", g=NG).unsqueeze(3).broadcast_to([P, NT, NG, NG])
            link(v.tensor_tensor(gr[:], gj, gi, ALU.is_gt))
            link(v.tensor_tensor(gr2, gj, gi, ALU.is_equal))
            link(v.tensor_tensor(gr2, gr2, before[:].unsqueeze(1).broadcast_to([P, NT, NG, NG]), ALU.mult))
            link(v.tensor_tensor(gr[:], gr[:], gr2, ALU.add))
            link(v.tensor_reduce(g2[:], gr[:].rearrange("p t i j -> p (t i) j"), AX.X, ALU.add))
            link(v.tensor_scalar(g2[:], g2[:], float(TG), None, ALU.is_lt))
            link(v.tensor_scalar(g2[:], g2[:], -1.0, NEG, ALU.add, ALU.mult))
            link(v.tensor_tensor(groups_of(R[3]), groups_of(R[1]), per_group(g2), ALU.add))
            for t in range(NT):
                link(v.max(t8[:, t], R[3][:, t]))
            eighth = t8[:, :, 7:8].broadcast_to([P, NT, NE])
            link(v.tensor_tensor(R[4], R[3], eighth, ALU.is_gt))
            link(v.tensor_tensor(R[5], R[3], eighth, ALU.is_equal))
            link(v.tensor_reduce(s4[:], R[4], AX.X, ALU.add))
            link(v.tensor_scalar(s4[:], s4[:], -1.0, float(TK), ALU.mult, ALU.add))
            link(v.tensor_tensor_scan(flat(R[6]), keep[:, 0:NT * NE], flat(R[5]), 0.0, ALU.mult, ALU.add))
            link(v.tensor_tensor(R[6], R[6], per_tile(s4[:]), ALU.is_le))
            link(v.tensor_tensor(R[5], R[5], R[6], ALU.mult))
            v.tensor_tensor(R[4], R[4], R[5], ALU.add).then_inc(S["ro_sel"], 1)
            dve.wait_ge(S["ro_sel"], 1)
            link(v.tensor_tensor(R[5], R[0], R[4], ALU.mult))
            link(v.tensor_reduce(s5[:], R[5], AX.X, ALU.add))
            link(v.reciprocal(s5[:], s5[:]))
            link(v.tensor_tensor(R[5], R[5], per_tile(s5[:]), ALU.mult))

            def column(c):
                return meta[:, :, :, c].rearrange("p e t -> p t e")

            link(v.tensor_scalar(column(2), R[5], ROUTED_SCALE, None, ALU.mult))
            link(v.tensor_scalar(s4[:], tok_id[:], -BIG, None, ALU.add))
            link(v.tensor_copy(column(0), per_tile(s4[:])))
            link(v.tensor_scalar(s5[:], tok_id[:], float(TK), -BIG - 1.0, ALU.mult, ALU.add))
            link(v.tensor_tensor_scan(flat(R[6]), keep[:, 0:NT * NE], flat(R[4]), 0.0, ALU.mult, ALU.add))
            link(v.tensor_tensor(column(1), R[6], per_tile(s5[:]), ALU.add))
            dve.wait_ge(S["pos_m"], 1)
            link(v.scalar_tensor_tensor(R[6], ps[:, 7, 0:NT * NE].rearrange("p (t e) -> p t e", e=NE), 1.0,
                                        R[4], ALU.add, ALU.mult))
            for c in range(MAXC):
                v.tensor_scalar(pos_x[:, c * NE:(c + 1) * NE, :].rearrange("p e t -> p t e"), R[6],
                                -1.0 - CAP * c, None, ALU.add)
            link(v.tensor_reduce(n_max[:, 0:1], ps[:, 7, NT * NE:(NT + 1) * NE], AX.X, ALU.max))
            link(v.tensor_scalar(n_max[:, 1:2], n_max[:, 0:1], float(CAP), None, ALU.is_gt))
            for c in range(2, MAXC):
                link(v.scalar_tensor_tensor(n_max[:, c:c + 1], n_max[:, 0:1], float(CAP * c), n_max[:, c - 1:c],
                                            ALU.is_gt, ALU.add))
            v.tensor_scalar(n_int[:], n_max[:, MAXC - 1:MAXC], float(GROUPS), float(GROUPS - 2), ALU.mult, ALU.add)\
                .then_inc(S["nch_ready"], 1)

            dve.wait_ge(S["nch_ready"], 1)
            n_mid = dve.value_load(n_int[0:1, 0:1], min_val=GROUPS - 2, max_val=GROUPS * MAXC - 2)

            def placed(i, u, early=False):
                if not early:
                    dve.wait_ge(S["idxm"], i - 1)
                at_i = pos_x[:, i, :] if isinstance(i, int) else \
                    pos_x[:, bass.ds(i, 1), :].rearrange("p o t -> p (o t)")
                v.tensor_tensor(place[:, i2(u)], slot_id[:, 0:CAP].unsqueeze(1).broadcast_to([P, NT, CAP]),
                                at_i.unsqueeze(2).broadcast_to([P, NT, CAP]), ALU.is_equal).then_inc(S["place_v"], 1)

            def indices(i, u):
                dve.wait_ge(S["idxm"], i + 1)
                if not isinstance(i, int) or i >= SLOTS:
                    dve.wait_ge(S["xt_m"], i + (1 - SLOTS))
                    dve.wait_ge(S["h_v"], i + (1 - SLOTS))
                v.tensor_copy(slot_v[0:CAP, u], ps[0:CAP, 7, 1:3])
                v.tensor_scalar(idx_g[0:CAP, u:u + 1], ps[0:CAP, 7, 0:1], BIG, None, ALU.add).then_inc(S["idx_v"], 1)

            def hidden(i, u, n, early):
                dve.wait_ge(S["idx_v"], i + 1)
                if not isinstance(n, int):
                    dve.wait_ge(Y_ST[u], n * 16)
                v.tensor_scalar(idx_s[0:CAP, u:u + 1], slot_v[0:CAP, u, 0:1], BIG, None, ALU.add)
                dve.wait_ge(S["si_a"], i + 1)
                if not early:
                    dve.wait_ge(S["ht_m"], i - 1)
                v.scalar_tensor_tensor(h_e[0:CAP, i2(u)], ps[0:CAP, 2 + i2(u), DE:2 * DE], slot_v[0:CAP, u, 1:2],
                                       silu_g[0:CAP, i2(u)], ALU.mult, ALU.mult).then_inc(S["h_v"], 1)

            def y_half(i, u, stored):
                dve.wait_ge(S["dn_m"], i + 1)
                if stored is not None:
                    dve.wait_ge(Y_ST[u], stored)
                v.tensor_copy(y_sb[0:CAP, u, 512:1024], ps[0:CAP, 6, :]).then_inc(S["y_v"], 1)

            def group(i0, n, first=False, last=False):
                for u in range(SLOTS):
                    if not (last and u >= 1):
                        indices(i0 + (u + 3), (u + 3) % SLOTS)
                    if not last:
                        placed(i0 + (u + 4), u)
                    hidden(i0 + u, u, n, first and u < 2)
                    if not (first and u == 0):
                        y_half(i0 + (u - 1), (u + 3) % SLOTS, stored_before(u, n, first))

            placed(0, 0, True)
            placed(1, 1, True)
            dve.wait_ge(S["st_h"], 16 * NT)
            for t in range(2):
                shared_y(t)
                shared_h(t + 2)
            indices(0, 0)
            placed(2, 2)
            indices(1, 1)
            placed(3, 3)
            indices(2, 2)
            for t in range(2, NT):
                shared_y(t)
            group(0, 0, first=True)
            with dve.Fori(1, n_mid + 1) as n:
                group(dve.snap(n * SLOTS), n)
            i0 = dve.snap(n_mid * SLOTS + SLOTS)
            n_last = dve.snap(n_mid + 1)
            group(i0, n_last, last=True)
            y_half(i0 + 3, 3, n_last * 16)
            for t in range(NT):
                dve.wait_ge(S[f"y_ld{t % 2}"], 16 * (t // 2 + 1))
                v.tensor_reduce(y_sum[:, t % 2], y_in[:, t % 2].rearrange("p k d -> p d k"), AX.X, ALU.add)\
                    .then_inc(S["fin_v"], 1)
                dve.wait_ge(S["fin_v"], t + 1)
                link(v.tensor_tensor(acc[:, t], acc[:, t], y_sum[:, t % 2], ALU.add))
                link(v.bn_stats(stats[:, 0], acc[:, t, 0:512]))
                link(v.bn_stats(stats[:, 1], acc[:, t, 512:1024]))
                v.bn_aggr(mv[:, t], stats[:]).then_inc(S["ln2v_v"], 1)
                dve.wait_ge(S["ln2s_a"], t + 1)
                link(v.reciprocal(rs[:, t:t + 1], rs[:, t:t + 1]))
                v.tensor_scalar(acc[:, t], acc[:, t], mv[:, t, 0:1], rs[:, t:t + 1], ALU.subtract, ALU.mult)\
                    .then_inc(S["ln2n_v"], 1)

        @block.tensor
        def _(pe):
            m = nc.tensor.matmul
            pe.wait_ge(S["consts"], 1)
            for t in range(NT):
                pe.wait_ge(S[f"ld_x{t}"], 16)
                xv = x_nat[:, t].rearrange("p (c k) -> p k c", k=KD)
                for half in range(2):
                    o = pe_unit(pe, f"xt{t}{half}")
                    for k in range(4):
                        last = nc.tensor.transpose(o[:, k * P:(k + 1) * P], xv[:, 4 * half + k], ident[:])
                    last.then_inc(S["units"], 1)
            pe.wait_ge(S["xT_a"], NT)
            pe.wait_ge(S["xT_v"], NT)

            def project(name, w):
                o = pe_unit(pe, name)
                for k in range(KD):
                    last = m(o, w[:, k], xT[:, k], start=k == 0, stop=k == KD - 1)
                last.then_inc(S["units"], 1)

            pe.wait_ge(S["ld_lat"], 48)
            project("cq0", w_lat[:, :, 0:128])
            project("cq1", w_lat[:, :, 128:256])
            project("ckv", w_lat[:, :, 256:384])
            project("kidx", w_lat[:, :, 384:512])
            o = pe_unit(pe, "widx")
            for t in range(NT):
                for k in range(KD):
                    last = m(o[:, t * IH:(t + 1) * IH], xT[:, k, t * P:(t + 1) * P], w_lat[:, k, 512:516],
                             start=k == 0, stop=k == KD - 1)
            last.then_inc(S["units"], 1)

            def f_unit(h):
                if h % 2 == 0:
                    pe.wait_ge(S[f"ld_blk{h // 2}"], 16)
                project(f"hf{h}", w_blk[h // 2][:, :, (h % 2) * DK:(h % 2 + 1) * DK])

            def across(name, parts):
                o = pe_unit(pe, name)
                for i, part in enumerate(parts):
                    last = m(o, ones[:], part, start=i == 0, stop=i == len(parts) - 1)
                last.then_inc(S["units"], 1)

            f_unit(0)
            pe.wait_ge(S["consts"], 2)
            pe.wait_ge(S["lat_a"], 3)
            across("ss_cq", [sq[:, 0], sq[:, 1]])
            across("ss_ckv", [sq[:, 2]])
            pe.wait_ge(S["kx_a"], 1)
            across("mean_k", [kxT])
            f_unit(1)
            pe.wait_ge(S["sqk_a"], 1)
            across("var_k", [sqk])
            f_unit(2)

            def up(name, w, src, n):
                o = pe_unit(pe, name)
                for k in range(n):
                    last = m(o, w[k], src[k], start=k == 0, stop=k == n - 1)
                last.then_inc(S["units"], 1)

            pe.wait_ge(S["ld_up"], 48)
            pe.wait_ge(S["norm_v"], 3)
            up("qidx0", [wqi_up[:, k, 0:P] for k in range(2)], [cqT[:, 0], cqT[:, 1]], 2)
            f_unit(3)
            up("qidx1", [wqi_up[:, k, P:2 * P] for k in range(2)], [cqT[:, 0], cqT[:, 1]], 2)

            def logits_of(t):
                for i in range(IH):
                    o = pe_unit(pe, f"lg{t}{i}")
                    lo = IDH * (i % 2)
                    m(o[:, 0:(t + 1) * P], qiT[lo:lo + IDH, i // 2, t * P:(t + 1) * P],
                      kxT[lo:lo + IDH, 0:(t + 1) * P], start=True, stop=True).then_inc(S["units"], 1)

            pe.wait_ge(S["qidx_a"], 2)
            pe.wait_ge(S["kn_v"], 1)
            logits_of(1)
            for j in range(4):
                up(f"qu{j}", [wq_up[:, k, j * P:(j + 1) * P] for k in range(2)], [cqT[:, 0], cqT[:, 1]], 2)
            for j in range(4):
                up(f"ku{j}", [wkv_up[:, j * P:(j + 1) * P]], [ckT], 1)
            logits_of(2)
            for t in range(NT):
                up(f"vu{t}", [ckT[:, t * P:(t + 1) * P]], [wkv_up[:, AW:2 * AW]], 1)
            for h in range(HG):
                if h % 2 == 0:
                    pe.wait_ge(S[f"ld_blk{h // 2}"], 32)
                project(f"hq{h}", w_blk[h // 2][:, :, (h % 2) * DK:(h % 2 + 1) * DK])
            logits_of(3)
            for name, done in (("hi", 48), ("hg", 64)):
                for b in range(2):
                    pe.wait_ge(S[f"ld_blk{b}"], done)
                    for t in range(NT):
                        o = pe_unit(pe, f"{name}{b}{t}")
                        for k in range(KD):
                            last = m(o[:, 0:256], xT[:, k, t * P:(t + 1) * P], w_blk[b][:, k],
                                     start=k == 0, stop=k == KD - 1)
                        last.then_inc(S["units"], 1)

            for h in range(HG + 1):
                if h < HG:
                    pe.wait_ge(S["dec_p"], h + 1)
                    o = pe_unit(pe, f"kd{h}")
                    for t in range(NT):
                        last = nc.tensor.transpose(o[:, t * P:(t + 1) * P], lf[:, h, t * P:(t + 1) * P], ident[:])
                    last.then_inc(S["units"], 1)
                    o = pe_unit(pe, f"sc{h}")
                    for t in range(NT):
                        last = m(o[:, t * P:(t + 1) * P], enb[:, h, t * P:(t + 1) * P], qs[:, h, t * P:(t + 1) * P],
                                 start=True, stop=True)
                    last.then_inc(S["units"], 1)
                    pe.wait_ge(S["kd_a"], h + 1)
                    pe.wait_ge(S["vh_a"], 2 * NT)
                    for odd in range(2):
                        o = pe_unit(pe, f"ds{'ab'[odd]}{h}")
                        lo = CHUNK * odd
                        for t in range(NT - odd):
                            last = m(o[:, t * DV:(t + 1) * DV], kdN[lo:lo + CHUNK, h, t * P:(t + 1) * P],
                                     v_hg[lo:lo + CHUNK, t, h * DV:(h + 1) * DV], start=True, stop=True)
                        last.then_inc(S["units"], 1)
                if h:
                    g = h - 1
                    pe.wait_ge(S["sc_p"], g + 1)
                    pe.wait_ge(S["st_v"], 7 * g + 7)
                    o = pe_unit(pe, f"o{g}")
                    for t in range(NT):
                        last = m(o[:, t * DV:(t + 1) * DV], sT[:, g, t * P:(t + 1) * P],
                                 v_hg[:, t, g * DV:(g + 1) * DV], start=True, stop=False, skip_group_check=True)
                        for c in (2 * t, 2 * t + 1):
                            if c:
                                lo = CHUNK * (c % 2)
                                last = m(o[lo:lo + CHUNK, t * DV:(t + 1) * DV], qs[:, g, c * CHUNK:(c + 1) * CHUNK],
                                         states[:, g % 2, c], start=False, stop=True, skip_group_check=True)
                    last.then_inc(S["units"], 1)

            def scores(i):
                t, h = pairs[i]
                if i == 0:
                    pe.wait_ge(S["up_a"], 12)
                o = pe_unit(pe, "S%d%d" % (t, h))
                lo = DH * (h % 2)
                m(o[:, 0:(t + 1) * P], qT[lo:lo + DH, h // 2, t * P:(t + 1) * P], kT[lo:lo + DH, h // 2, 0:(t + 1) * P],
                  start=True, stop=True).then_inc(S["units"], 1)

            def probs_t(i):
                t, h = pairs[i]
                pe.wait_ge(S["norm2_v"], i + 1)
                o = pe_unit(pe, "PT%d%d" % (t, h))
                for j in range(t + 1):
                    last = nc.tensor.transpose(o[:, j * P:(j + 1) * P], at_p[:, i % 2, j * P:(j + 1) * P], ident[:])
                last.then_inc(S["units"], 1)

            def values(i):
                t, h = pairs[i]
                o = pe_unit(pe, f"PV{t}{h // 2}")
                pe.wait_ge(S["pT_a"], i + 1)
                for g in (0, 1):
                    for j in range(t + 1):
                        last = m(o[DH * g:DH * g + DH, 0:P], v_at[:, j, (h - 1 + g) * DH:(h + g) * DH],
                                 at_pT[:, g, j * P:(j + 1) * P], start=j == 0, stop=j == t)
                last.then_inc(S["units"], 1)

            def mix_out(t, half):
                pe.wait_ge(S["ld_wo"], 16)
                pe.wait_ge(S["pv_a"], 4 * (t + 1))
                pe.wait_ge(S["oT_a"], HG)
                o = pe_unit(pe, f"out{t}{half}")
                for k in range(KD):
                    last = m(o, oT[:, k, t * P:(t + 1) * P], w_o[:, k, half * 512:(half + 1) * 512],
                             start=k == 0, stop=k == KD - 1)
                last.then_inc(S["units"], 1)

            def mix_a_t(h):
                pe.wait_ge(S["oa_v"], h + 1)
                o = pe_unit(pe, f"oaT{h}")
                for t in range(NT):
                    last = nc.tensor.transpose(o[:, t * P:(t + 1) * P], mix_a[:, h, t * P:(t + 1) * P], ident[:])
                last.then_inc(S["units"], 1)

            for i in range(len(pairs) + 3):
                if i < len(pairs):
                    t, h = pairs[i]
                    scores(i)
                    if t and h in (3, 6):
                        mix_out(t - 1, h // 6)
                    if t == 0 and h in (2, 3, 4, 5):
                        mix_a_t(h - 2)
                if 0 <= i - 2 < len(pairs):
                    probs_t(i - 2)
                if 0 <= i - 3 < len(pairs) and pairs[i - 3][1] % 2:
                    values(i - 3)
            for half in range(2):
                mix_out(NT - 1, half)

            def normed_rows(t):
                pe.wait_ge(S["lng_p"], 2 * t + 2)
                hv = acc[:, t].rearrange("p (c k) -> p k c", k=KD)
                for half in range(2):
                    o = pe_unit(pe, f"hT{t}{half}")
                    for k in range(4):
                        last = nc.tensor.transpose(o[:, k * P:(k + 1) * P], hv[:, 4 * half + k], ident[:])
                    last.then_inc(S["units"], 1)
                pe.wait_ge(S["hT_v"], t + 1)
                pe.wait_ge(S["hT_a"], t + 1)
                o = pe_unit(pe, f"rl{t}")
                for k in range(KD):
                    last = m(o[:, 0:NE], hT[:, k, t * P:(t + 1) * P], w_rt[:, k], start=k == 0, stop=k == KD - 1)
                last.then_inc(S["units"], 1)

            def transposed_hidden(o, h_row, n):
                hv = h_row.rearrange("p (c k) -> p k c", k=2)
                for k in range(2):
                    last = nc.tensor.transpose(o[:, k * n:(k + 1) * n], hv[:, k], ident[0:n, 0:n])
                return last

            def down(o, hid_t, w, half, n):
                for k in range(2):
                    last = m(o, hid_t[:, k * n:(k + 1) * n], w[:, k, half * 512:(half + 1) * 512],
                             start=k == 0, stop=k == 1)
                return last

            def shared_gate_up(t):
                o = pe_unit(pe, f"sg{t}")
                for k in range(KD):
                    last = m(o, hT[:, k, t * P:(t + 1) * P], ws_gu[:, :, k], start=k == 0, stop=k == KD - 1)
                last.then_inc(S["units"], 1)

            def shared_down(t):
                o = pe_unit(pe, f"st{t}")
                pe.wait_ge(S["sh_h"], t + 1)
                transposed_hidden(o, h_e[:, t % 2], P).then_inc(S["units"], 1)
                pe.wait_ge(S["sh_t"], t + 1)
                for half in range(2):
                    o = pe_unit(pe, f"sd{t}{half}")
                    down(o, heT[:, t % 2], ws_dn, half, P).then_inc(S["units"], 1)

            pe.wait_ge(S["ld_rt"], 16)
            for t in range(NT - 1):
                normed_rows(t)
            pe.wait_ge(S["ld_sgu"], 32)
            pe.wait_ge(S["ld_sdn"], 16)
            shared_gate_up(0)
            normed_rows(NT - 1)
            for t in range(1, NT):
                shared_gate_up(t)
            pe.wait_ge(S["ro_sel"], 1)
            for q in range(NT):
                for j in range(q + 1):
                    m(ps[:, 7, q * NE:(q + 1) * NE], lower[:] if j == q else ones[:], R[4][:, j],
                      start=j == 0, stop=j == q)
            for j in range(NT):
                last = m(ps[:, 7, NT * NE:(NT + 1) * NE], ones[:], R[4][:, j], start=j == 0, stop=j == NT - 1)
            last.then_inc(S["pos_m"], 1)
            for t in range(2):
                shared_down(t)

            pe.wait_ge(S["nch_ready"], 1)
            n_mid = pe.value_load(n_int[0:1, 0:1], min_val=GROUPS - 2, max_val=GROUPS * MAXC - 2)

            def slots_of(i, e, u, early=False):
                pe.wait_ge(S["place_v"], i + 1)
                if not early:
                    pe.wait_ge(S["idx_v"], i)
                for t in range(NT):
                    row = meta[:, e, t, :] if isinstance(e, int) else \
                        meta[:, bass.ds(e, 1), t, :].rearrange("p o j -> p (o j)")
                    last = m(ps[0:CAP, 7, 0:3], place[:, i2(u), t], row, start=t == 0, stop=t == NT - 1)
                last.then_inc(S["idxm"], 1)

            def rows_t(i, u, gathers, early=False):
                pe.wait_ge(X_GA[u % SLOTS], gathers)
                if not early:
                    pe.wait_ge(S["xt_e"], i)
                xv = xg[0:CAP, u % SLOTS].rearrange("p (c k) -> p k c", k=KD)
                for k in range(KD):
                    last = nc.tensor.transpose(ps[:, k // 4, (k % 4) * CAP:(k % 4 + 1) * CAP], xv[:, k],
                                               ident[0:CAP, 0:CAP])
                last.then_inc(S["xt_m"], 1)

            def gate_up(i, u, loads, early=False):
                pe.wait_ge(S["xt_e"], i + 1)
                if not early:
                    pe.wait_ge(S["h_v"], i - 1)
                pe.wait_ge(W_GU[u], loads)
                for k in range(KD):
                    last = m(ps[0:CAP, 2 + i2(u), :], xgT[:, i2(u), k * CAP:(k + 1) * CAP], w_gu[u][:, :, k],
                             start=k == 0, stop=k == KD - 1)
                last.then_inc(S["gu_m"], 1)

            def hidden_t(i, u, early=False):
                pe.wait_ge(S["h_v"], i + 1)
                if not early:
                    pe.wait_ge(S["ht_a"], i)
                transposed_hidden(ps[:, 4, :], h_e[0:CAP, i2(u)], CAP).then_inc(S["ht_m"], 1)

            def down_rows(i, u, loads, early=False):
                pe.wait_ge(S["ht_a"], i + 1)
                if not early:
                    pe.wait_ge(S["y_a"], i)
                    pe.wait_ge(S["y_v"], i)
                pe.wait_ge(W_DN[u], loads)
                for half in range(2):
                    last = down(ps[0:CAP, 5 + half, :], heT_x[:, i2(u)], w_dn[u], half, CAP)
                last.then_inc(S["dn_m"], 1)

            def group(i0, n, e0, e_next, first=False, last=False):
                for u in range(SLOTS):
                    if not (last and u == SLOTS - 1):
                        rows_t(i0 + (u + 1), u + 1, (n + (u + 1) // SLOTS + 1) * 16)
                    prev = n if u else n - 1
                    if not (first and u == 0):
                        hidden_t(i0 + (u - 1), u + 3, first and u == 1)
                    if not (last and u >= 1):
                        slots_of(i0 + (u + 3), (e_next if u else e0) + (u + 3) % SLOTS, u + 3)
                    gate_up(i0 + u, u, (n + 1) * 32, first and u < 2)
                    if not (first and u == 0):
                        down_rows(i0 + (u - 1), (u + 3) % 4, (prev + 1) * 16, first and u == 1)

            slots_of(0, 0, 0, True)
            slots_of(1, 1, 1)
            slots_of(2, 2, 2)
            for t in range(2, NT):
                shared_down(t)
            pe.wait_ge(S["sh_y"], 2 * NT)
            rows_t(0, 0, 16, True)
            group(0, 0, 0, SLOTS, first=True)
            with pe.Fori(1, n_mid + 1) as n:
                group(pe.snap(n * SLOTS), n, pe.snap((n % GROUPS) * SLOTS), pe.snap(((n + 1) % GROUPS) * SLOTS))
            n_last = pe.snap(n_mid + 1)
            i0 = pe.snap(n_last * SLOTS)
            group(i0, n_last, NE - SLOTS, None, last=True)
            hidden_t(i0 + 3, 3)
            down_rows(i0 + 3, 3, (n_last + 1) * 16)


_INS = ["x", "w_in", "hg_lb_logits", "hg_norm_g", "q_norm_g", "w_q_up", "w_qidx_up", "kv_norm_g", "w_kv_up",
        "idx_ln_g", "idx_ln_b", "w_out", "ln1_g", "ln1_b", "w_router", "router_bias", "w_e_gate", "w_e_up",
        "w_e_down", "w_s_gate", "w_s_up", "w_s_down", "ln2_g", "ln2_b"]


def kernel(**inputs):
    import numpy as _np
    import concourse.bacc as _bacc
    from concourse.bass_utils import run_bass_kernel_spmd as _run

    nc = _bacc.Bacc("TRN2", target_bir_lowering=False, num_devices=1)
    arrays, args = {}, []
    for name in _INS:
        a = _np.ascontiguousarray(inputs[name])
        arrays[f"in_{name}"] = a
        args.append(nc.dram_tensor(f"in_{name}", a.shape, mybir.dt.from_np(a.dtype), kind="ExternalInput").ap())
    args.append(nc.dram_tensor("out_0", (1, SEQ, DM), F32, kind="ExternalOutput").ap())
    hybrid_block(nc, *args)
    r = _run(nc, [arrays], core_ids=[0])
    return r.results[0]["out_0"]
```

```python
from contextlib import ExitStack

import concourse.bass as bass
from concourse import mybir

ALU = mybir.AluOpType
ACT = mybir.ActivationFunctionType
AX = mybir.AxisListType
F32 = mybir.dt.float32
I32 = mybir.dt.int32
BF16 = mybir.dt.bfloat16

P = 128
SEQ, DM = 512, 1024
NT = SEQ // P
KD = DM // P
CHUNK = 64
NCH = SEQ // CHUNK
HG, DK, DV = 4, 128, 128
AH, DH = 8, 64
AW = AH * DH
QR, KVR = 256, 128
IH, IDH = 4, 64
TOPK = 128
NE, TK, NG, TG = 64, 8, 8, 4
PER = NE // NG
DE = 256
ROUTED_SCALE = 2.5
ALPHA = 2.0 ** 0.25
LN_EPS, RMS_EPS = 1e-5, 1e-6
CQ0 = 2048
BIG = 16384.0
NEG = 1e30
CAP = 96
MAXC = -(-SEQ // CAP)
RING = 7
SLOTS = 4
GROUPS = NE // SLOTS


def hybrid_block(nc, x, w_in, hg_lb_logits, hg_norm_g, q_norm_g, w_q_up, w_qidx_up, kv_norm_g, w_kv_up,
                 idx_ln_g, idx_ln_b, w_out, ln1_g, ln1_b, w_router, router_bias, w_e_gate, w_e_up,
                 w_e_down, w_s_gate, w_s_up, w_s_down, ln2_g, ln2_b, out):
    h_rows = nc.dram_tensor("h_rows", (SEQ, DM), F32).ap()
    y_rows = nc.dram_tensor("y_rows", (SEQ * TK, DM), F32).ap()

    with ExitStack() as ctx:
        def sb(name, shape, dt=F32):
            return ctx.enter_context(nc.sbuf_tensor(name, shape, dt))

        def sem(name):
            return ctx.enter_context(nc.semaphore(name))

        WORDS = 50432
        arena = sb("arena", [P, WORDS])

        def at(start, *shape):
            n = 1
            for d in shape:
                n *= d
            v = arena[:, start:start + n]
            if len(shape) == 1:
                return v
            names = " ".join(f"d{i}" for i in range(len(shape)))
            return v.rearrange(f"p ({names}) -> p {names}", **{f"d{i}": s for i, s in enumerate(shape[:-1])})

        EW = KD * 2 * DE + 2 * DM
        SLOT_AT = [0, EW, 2 * EW, 22528]
        w_gu = [at(s, 2, KD, DE) for s in SLOT_AT]
        w_dn = [at(s + KD * 2 * DE, 2, DM) for s in SLOT_AT]
        w_lat = at(6144, KD, 516)
        w_blk = [at(10272, KD, 256), at(12320, KD, 256)]
        w_o = at(6144, KD, DM)
        lf = at(14368, HG, SEQ)
        o_hg = lf
        wq_up = at(16416, 2, 512)
        wqi_up = at(17440, 2, 256)
        x_nat = at(18432, NT, DM)
        xT = at(22528, KD, SEQ)
        oT = xT
        qT = at(26624, 4, SEQ)
        kT = at(28672, 4, SEQ)
        v_at = at(30720, NT, AW)
        MASK_AT = [32768, 32896, 33152, 33536]
        sel_mask = [at(MASK_AT[t], (t + 1) * P) for t in range(NT)]
        kf = at(34048, HG, SEQ)
        sT = kf
        enb = at(36096, HG, SEQ)
        mix_a = enb
        eb = at(38144, HG, SEQ)
        kdN = eb
        qs = at(40192, HG, SEQ)
        v_hg = at(42240, NT, HG * DV)
        gate = at(44288, NT, HG * DV)
        wkv_up = at(46336, 2 * AW)
        cqT = at(47360, 2, SEQ)
        ckT = at(48384, SEQ)
        kxT = at(48896, SEQ)
        qiT = at(49408, 2, SEQ)
        states = at(46336, 2, NCH, DV)
        sq = at(18432, 3, SEQ)
        rt = at(18432 + 1536, 3, SEQ)
        sqk = at(18432 + 3072, SEQ)
        score = at(18432, SEQ)
        work = at(18432 + 512, SEQ)
        m_eq = at(18432 + 1024, SEQ)
        m_cum = at(18432 + 1536, SEQ)
        relu_t = at(18432 + 2048, 2, SEQ)
        at_bias = at(18432, 2, SEQ)
        at_s = at(18432 + 1024, 2, SEQ)
        at_p = at(18432 + 2048, 2, SEQ)
        at_pT = at(18432 + 3072, 2, SEQ)
        acc = at(34048, NT, DM)
        ln_g = at(18432, DM)
        ln_b = at(18432 + 1024, DM)
        hT = at(38144, KD, SEQ)
        ws_gu = at(42240, 2, KD, DE)
        ws_dn = at(46336, 2, DM)
        silu_g = at(48384, 2, DE)
        h_e = at(48896, 2, DE)
        heT = at(49408, 2, DE)
        heT_x = at(49408, 2, 2 * CAP)
        R = [at(18432 + 2048 + 256 * i, NT, NE) for i in range(8)]
        w_rt = at(33536, KD, NE)
        pos_x = at(28672, MAXC * NE, NT)
        META = 9
        meta_at = 28672 + MAXC * NE * NT
        meta = arena[:, meta_at:meta_at + NE * NT * META // 2].bitcast(BF16)\
            .rearrange("p (e t j) -> p e t j", e=NE, t=NT)
        place = arena[:, 32768:32768 + NT * CAP].bitcast(BF16).rearrange("p (b t c) -> p b t c", b=2, t=NT)
        xg = at(38144, SLOTS, DM)
        xgT = at(42240, 2, KD * CAP)
        y_sb = at(44288, SLOTS, DM)
        y_in = at(0, 2, TK, DM)

        ident = sb("ident", [P, P])
        ones = sb("ones", [P, P])
        lower = sb("lower", [P, P])
        dist = sb("dist", [P, SEQ])
        keep = sb("keep", [P, SEQ])
        slot_id = sb("slot_id", [P, P])
        tok_id = sb("tok_id", [P, NT])
        norm_row = sb("norm_row", [P, DV])
        bias_row = sb("bias_row", [P, NE])
        before = sb("before", [P, NG, NG])
        lbl = sb("lbl", [P, 2, HG])
        lb = sb("lb", [P, HG])
        one_lb = sb("one_lb", [P, HG])
        gq = sb("gq", [P, 2])
        gkv = sb("gkv", [P, 1])
        gk = sb("gk", [P, 1])
        bk = sb("bk", [P, 1])
        w_i = sb("w_i", [P, NT, IH])
        top8 = sb("top8", [P, 8])
        cnt = sb("cnt", [P, 2])
        dec = sb("dec", [P, HG, NCH])
        ss_o = sb("ss_o", [P, HG, NT])
        r_o = sb("r_o", [P, HG, NT])
        nmax = sb("nmax", [P, AH * NT])
        rsum = sb("rsum", [P, AH * NT])
        rinv = sb("rinv", [P, AH * NT])
        stats = sb("stats", [P, 2, 6])
        mv = sb("mv", [P, NT, 2])
        rs = sb("rs", [P, NT])
        eps_t = sb("eps_t", [P, 2])
        g1 = sb("g1", [P, NT * NG])
        g2 = sb("g2", [P, NT * NG])
        g3 = sb("g3", [P, NT * NG])
        gr = sb("gr", [P, NT, NG, NG])
        gr2 = at(32768, NT, NG, NG)
        t8 = sb("t8", [P, NT, 8])
        s4 = sb("s4", [P, NT])
        s5 = sb("s5", [P, NT])
        n_max = sb("n_max", [P, MAXC])
        n_int = sb("n_int", [P, 1], I32)
        idx_g = sb("idx_g", [P, SLOTS], I32)
        idx_s = sb("idx_s", [P, SLOTS], I32)
        slot_v = sb("slot_v", [P, SLOTS, 3])

        ps = ctx.enter_context(nc.psum_tensor("ps", [P, 8, 512], F32))

        names = """ld_x0 ld_x1 ld_x2 ld_x3 ld_cq0 ld_lat ld_blk0 ld_blk1 ld_small ld_up ld_wo ld_xr ld_ln
            ld_ln2 ld_rt ld_sgu ld_sdn consts const_step units xT_a xT_v lat_a kx_a wi_v sig_a f_v lnf_a
            sqrt_a norm_v xc_v sqk_a kn_v qidx_a relu_a idxs_v up_a mask_v exp_a dec_p qs_a vh_a gate_a
            gate_p bsum_v kd_a sc_a sc_p st_v o_a sq_a rsq_a oa_v oT_a biasd_v prob_a norm2_v pT_a pv_a
            res_v lnv_v lns_a lnn_v st_h hT_a hT_v rl_a sh_si sh_h sh_t sh_y pos_m nch_ready link_v
            link_p lb_v lb_a place_v idxm slot_r idx_v turn_p xg_clear ln2n_v ln2v_v xt_m ht_a ro_sel
            xt_e gu_m si_a h_v ht_m dn_m y_a y_v ln2s_a fin_v pair_p fin_h ln2r_a fin_p out_st y_ld00
            y_ld01 y_ld02 y_ld03 y_ld10 y_ld11 y_ld12 y_ld13""".split()
        S = {n: sem(n) for n in names}
        W_GU = [sem(f"ld_gu{s}") for s in range(SLOTS)]
        W_DN = [sem(f"ld_dn{s}") for s in range(SLOTS)]
        X_GA = [sem(f"gathered{s}") for s in range(SLOTS)]
        Y_ST = [sem(f"scattered{s}") for s in range(SLOTS)]

        units = []

        def unit(name, read_by, count):
            units.append((name, read_by, count))

        for t in range(NT):
            unit(f"xt{t}0", "xT_v", t + 1)
            unit(f"xt{t}1", "xT_a", t + 1)
        for n, name in enumerate(("cq0", "cq1", "ckv")):
            unit(name, "lat_a", n + 1)
        unit("kidx", "kx_a", 1)
        unit("widx", "wi_v", 1)
        unit("hf0", "sig_a", 1)
        unit("ss_cq", "sqrt_a", 1)
        unit("ss_ckv", "sqrt_a", 2)
        unit("mean_k", "xc_v", 1)
        unit("hf1", "sig_a", 2)
        unit("var_k", "sqrt_a", 3)
        unit("hf2", "sig_a", 3)
        unit("qidx0", "qidx_a", 1)
        unit("hf3", "sig_a", 4)
        unit("qidx1", "qidx_a", 2)

        def logits(t):
            for i in range(IH):
                unit(f"lg{t}{i}", "relu_a", IH * (t - 1) + i + 1)

        logits(1)
        for m in range(4):
            unit(f"qu{m}", "up_a", m + 1)
        for m in range(4):
            unit(f"ku{m}", "up_a", 4 + m + 1)
        for t in range(NT):
            unit(f"vu{t}", "up_a", 8 + t + 1)
        for h in range(HG):
            unit(f"hq{h}", "qs_a", h + 1)
            if h == 1:
                logits(2)
        logits(3)
        for b in range(2):
            for t in range(NT):
                unit(f"hi{b}{t}", "vh_a", NT * b + t + 1)
        for b in range(2):
            for t in range(NT):
                unit(f"hg{b}{t}", "gate_a", NT * b + t + 1)
        for h in range(HG + 1):
            if h < HG:
                unit(f"kd{h}", "kd_a", h + 1)
                unit(f"sc{h}", "sc_a", h + 1)
                unit(f"dsa{h}", "st_v", 7 * h + 7)
                unit(f"dsb{h}", "st_v", 7 * h + 6)
            if h:
                unit(f"o{h - 1}", "o_a", h)
        OUT_AT = (5, 7)
        MIX_AT = (1, 2, 3, 4)
        pairs = [(t, h) for t in range(NT) for h in range(AH)]
        for i in range(len(pairs) + 3):
            if i < len(pairs):
                unit("S%d%d" % pairs[i], "biasd_v", 2 * i + 2)
                t, h = pairs[i]
                if t and h in OUT_AT:
                    half = OUT_AT.index(h)
                    unit(f"out{t - 1}{half}", "res_v", 2 * (t - 1) + half + 1)
                if t == 0 and h in MIX_AT:
                    unit(f"oaT{MIX_AT.index(h)}", "oT_a", MIX_AT.index(h) + 1)
            if 0 <= i - 2 < len(pairs):
                unit("PT%d%d" % pairs[i - 2], "pT_a", i - 1)
            if 0 <= i - 3 < len(pairs) and pairs[i - 3][1] % 2:
                t, h = pairs[i - 3]
                unit(f"PV{t}{h // 2}", "pv_a", (i - 3) // 2 + 1)
        for half in range(2):
            unit(f"out{NT - 1}{half}", "res_v", 2 * (NT - 1) + half + 1)

        for t in range(NT + 1):
            if t < NT:
                unit(f"hT{t}0", "hT_v", t + 1)
                unit(f"hT{t}1", "hT_a", t + 1)
            if t:
                unit(f"rl{t - 1}", "rl_a", t)
        for t in range(NT):
            unit(f"sg{t}", "sh_h", t + 1)
        for t in range(NT):
            unit(f"st{t}", "sh_t", t + 1)
            unit(f"sd{t}0", "sh_y", 2 * t + 1)
            unit(f"sd{t}1", "sh_y", 2 * t + 2)
        FIN_ORDER = (0, 4, 5, 2, 6, 7)
        LAST_OF = (0, 2, 5, 7)
        number = {u[0]: n for n, u in enumerate(units)}

        def made(name):
            return number[name] + 1

        def bank(name):
            return ps[:, number[name] % RING, :]

        def pe_unit(pe, name):
            n = number[name]
            if n >= RING:
                _, read_by, count = units[n - RING]
                pe.wait_ge(S[read_by], count)
            return ps[:, n % RING, :]

        def i2(u):
            return u % 2

        def stored_before(u, n, first):
            if first or (u == 0 and isinstance(n, int) and n == 1):
                return None
            return n * 16 if u else (n - 1) * 16

        def linker(eng, which):
            n = [0]

            def link(ins):
                n[0] += 1
                ins.then_inc(S[which], 1)
                eng.wait_ge(S[which], n[0])
            return link

        block = ctx.enter_context(nc.Block())
        x2 = x.rearrange("b s d -> (b s) d")
        out2 = out.rearrange("b s d -> (b s) d")
        w_in_v = w_in[0].rearrange("(p k) c -> p k c", k=KD)
        gate_w = w_e_gate[0]
        up_w = w_e_up[0]
        down_w = w_e_down[0]

        @block.sync
        def _(sp):
            for t in range(NT):
                sp.dma_start(x_nat[:, t, :], x2[t * P:(t + 1) * P, :]).then_inc(S[f"ld_x{t}"], 16)
            sp.dma_start(w_lat[:, :, 0:P], w_in_v[:, :, CQ0:CQ0 + P]).then_inc(S["ld_cq0"], 16)
            sp.dma_start(w_lat[:, :, P:448], w_in_v[:, :, CQ0 + P:CQ0 + 448]).then_inc(S["ld_lat"], 16)
            sp.dma_start(w_lat[:, :, 448:512], w_in_v[:, :, CQ0 + 384:CQ0 + 448]).then_inc(S["ld_lat"], 16)
            sp.dma_start(w_lat[:, :, 512:516], w_in_v[:, :, CQ0 + 448:CQ0 + 452]).then_inc(S["ld_lat"], 16)
            cols = [512, 768, 0, 256, 1024, 1280, 1536, 1792]
            last_use = ["hf1", "hf3", "hq1", "hq3", "hi03", "hi13", "hg03", "hg13"]
            for j, c in enumerate(cols):
                if j >= 2:
                    sp.wait_ge(S["units"], made(last_use[j - 2]))
                sp.dma_start(w_blk[j % 2][:, :, :], w_in_v[:, :, c:c + 256]).then_inc(S[f"ld_blk{j % 2}"], 16)
                if j == 1:
                    sp.dma_start(wqi_up, w_qidx_up[0].rearrange("(m p) c -> p m c", p=P)).then_inc(S["ld_up"], 16)
                    sp.dma_start(wq_up, w_q_up[0].rearrange("(m p) c -> p m c", p=P)).then_inc(S["ld_up"], 16)
                    sp.dma_start(wkv_up, w_kv_up[0]).then_inc(S["ld_up"], 16)
                if j == 3:
                    sp.dma_start(w_gu[0][:, 0], gate_w[0].rearrange("(p k) f -> p k f", k=KD)).then_inc(W_GU[0], 16)
                    sp.dma_start(w_gu[0][:, 1], up_w[0].rearrange("(p k) f -> p k f", k=KD)).then_inc(W_GU[0], 16)
                    sp.dma_start(w_dn[0], down_w[0].rearrange("(p k) n -> p k n", k=2)).then_inc(W_DN[0], 16)
            sp.wait_ge(S["units"], made("hg13"))
            sp.dma_start(w_o, w_out[0].rearrange("(m p) n -> p m n", p=P)).then_inc(S["ld_wo"], 16)
            sp.wait_ge(S["oT_a"], HG)
            sp.dma_start(acc, x2.rearrange("(t p) d -> p t d", p=P)).then_inc(S["ld_xr"], 16)
            sp.wait_ge(S["o_a"], HG)
            sp.wait_ge(S["oT_a"], HG)
            sp.dma_start(ws_gu[:, 0], w_s_gate[0].rearrange("(p k) f -> p k f", k=KD)).then_inc(S["ld_sgu"], 16)
            sp.dma_start(ws_gu[:, 1], w_s_up[0].rearrange("(p k) f -> p k f", k=KD)).then_inc(S["ld_sgu"], 16)
            sp.dma_start(ws_dn, w_s_down[0].rearrange("(p k) n -> p k n", k=2)).then_inc(S["ld_sdn"], 16)
            sp.wait_ge(S["pv_a"], len(pairs) // 2)
            sp.dma_start(ln_g, ln1_g[0:1, :].broadcast_to([P, DM])).then_inc(S["ld_ln"], 16)
            sp.dma_start(ln_b, ln1_b[0:1, :].broadcast_to([P, DM])).then_inc(S["ld_ln"], 16)
            sp.dma_start(w_rt, w_router[0].rearrange("(p k) e -> p k e", k=KD)).then_inc(S["ld_rt"], 16)
            sp.wait_ge(S["units"], made(f"out{NT - 1}1"))

            def load_expert(e, s):
                sp.dma_start(w_gu[s][:, 0], gate_w[bass.ds(e, 1)].rearrange("e (p k) f -> (e p) k f", k=KD)).then_inc(W_GU[s], 16)
                sp.dma_start(w_gu[s][:, 1], up_w[bass.ds(e, 1)].rearrange("e (p k) f -> (e p) k f", k=KD)).then_inc(W_GU[s], 16)
                sp.dma_start(w_dn[s], down_w[bass.ds(e, 1)].rearrange("e (p k) n -> (e p) k n", k=2)).then_inc(W_DN[s], 16)

            def store_rows(t):
                sp.wait_ge(S["lnn_v"], t + 1)
                sp.dma_start(h_rows[t * P:(t + 1) * P, :], acc[:, t, :]).then_inc(S["st_h"], 16)

            load_expert(1, 1)
            for t in range(NT):
                store_rows(t)
            load_expert(2, 2)
            load_expert(3, 3)
            sp.dma_start(ln_g, ln2_g[0:1, :].broadcast_to([P, DM])).then_inc(S["ld_ln2"], 16)
            sp.dma_start(ln_b, ln2_b[0:1, :].broadcast_to([P, DM])).then_inc(S["ld_ln2"], 16)
            sp.wait_ge(S["nch_ready"], 1)
            n_mid = sp.value_load(n_int[0:1, 0:1], min_val=GROUPS - 2, max_val=GROUPS * MAXC - 2)
            with sp.Fori(1, n_mid + 2) as g:
                first = sp.snap((g % GROUPS) * SLOTS)
                for s in range(SLOTS):
                    gate_e = gate_w[bass.ds(first + s, 1)].rearrange("e (p k) f -> (e p) k f", k=KD)
                    up_e = up_w[bass.ds(first + s, 1)].rearrange("e (p k) f -> (e p) k f", k=KD)
                    down_e = down_w[bass.ds(first + s, 1)].rearrange("e (p k) n -> (e p) k n", k=2)
                    used = sp.snap(g * SLOTS + (s + 1 - SLOTS))
                    sp.wait_ge(S["gu_m"], used)
                    sp.dma_start(w_gu[s][:, 0], gate_e).then_inc(W_GU[s], 16)
                    sp.dma_start(w_gu[s][:, 1], up_e).then_inc(W_GU[s], 16)
                    sp.wait_ge(S["dn_m"], used)
                    sp.dma_start(w_dn[s], down_e).then_inc(W_DN[s], 16)
            items = sp.snap(n_mid * SLOTS + 2 * SLOTS)
            stored = sp.snap(n_mid * 16 + 32)
            sp.wait_ge(S["dn_m"], items)
            for s in range(SLOTS):
                sp.wait_ge(Y_ST[s], stored)
            y_v8 = y_rows.rearrange("(t p k) d -> t p k d", p=P, k=TK)
            for t in range(NT):
                for j in range(TK // 2):
                    if t >= 2:
                        sp.wait_ge(S["fin_v"], len(FIN_ORDER) * (t - 2) + FIN_ORDER.index(LAST_OF[j]) + 1)
                    sp.dma_start(y_in[:, t % 2, 2 * j:2 * j + 2], y_v8[t][:, 2 * j:2 * j + 2])\
                        .then_inc(S[f"y_ld{t % 2}{j}"], 16)
            for t in range(NT - 1):
                sp.wait_ge(S["fin_p"], t + 1)
                sp.dma_start(out2[t * P:(t + 1) * P, :], acc[:, t]).then_inc(S["out_st"], 16)
            for half in range(2):
                sp.wait_ge(S["fin_h"], half + 1)
                sp.dma_start(out2[(NT - 1) * P:NT * P, half * 512:(half + 1) * 512],
                             acc[:, NT - 1, half * 512:(half + 1) * 512]).then_inc(S["out_st"], 16)
            sp.wait_ge(S["out_st"], 16 * (NT + 1))

        @block.gpsimd
        def _(pool):
            link = linker(pool, "link_p")
            g = nc.gpsimd
            small = [
                (lbl[:], hg_lb_logits.rearrange("r (h p) -> p r h", p=P)),
                (gq[:], q_norm_g[0].rearrange("(m p) -> p m", p=P)),
                (gkv[:], kv_norm_g[0].rearrange("(p o) -> p o", o=1)),
                (gk[0:IDH, :], idx_ln_g[0].rearrange("(p o) -> p o", o=1)),
                (gk[IDH:P, :], idx_ln_g[0].rearrange("(p o) -> p o", o=1)),
                (bk[0:IDH, :], idx_ln_b[0].rearrange("(p o) -> p o", o=1)),
                (bk[IDH:P, :], idx_ln_b[0].rearrange("(p o) -> p o", o=1)),
                (norm_row[:], hg_norm_g[0:1, :].broadcast_to([P, DV])),
                (bias_row[:], router_bias[0:1, :].broadcast_to([P, NE])),
            ]
            g.memset(ident[:], 0.0).then_inc(S["const_step"], 1)
            g.memset(ones[:], 1.0)
            g.memset(keep[:], 1.0)
            g.memset(lower[:], 1.0)
            g.memset(before[:], 1.0)
            g.memset(eps_t[:, 0:1], RMS_EPS)
            g.memset(eps_t[:, 1:2], LN_EPS).then_inc(S["const_step"], 1)
            pool.wait_ge(S["const_step"], 2)
            g.affine_select(out=ident[:], in_=ident[:], compare_op=ALU.not_equal, fill=1.0, base=0,
                            pattern=[[-1, P]], channel_multiplier=1).then_inc(S["consts"], 1)
            for dst, src in small:
                pool.dma_start(dst, src, allow_slow_non_contiguous=True).then_inc(S["ld_small"], 16)
            g.affine_select(out=lower[:], in_=lower[:], compare_op=ALU.is_gt, fill=0.0, base=0,
                            pattern=[[1, P]], channel_multiplier=-1)
            g.affine_select(out=before[:], in_=before[:], compare_op=ALU.is_gt, fill=0.0, base=0,
                            pattern=[[1, NG], [-1, NG]], channel_multiplier=0)
            g.iota(dist[:], pattern=[[-1, SEQ]], base=SEQ - P, channel_multiplier=1,
                   allow_small_or_imprecise_dtypes=True)
            g.iota(slot_id[:], pattern=[[1, P]], base=0, channel_multiplier=0, allow_small_or_imprecise_dtypes=True)
            g.iota(tok_id[:], pattern=[[P, NT]], base=0, channel_multiplier=1, allow_small_or_imprecise_dtypes=True)
            g.memset(keep[:].rearrange("p (c s) -> p c s", s=CHUNK)[:, :, 0:1], 0.0).then_inc(S["consts"], 1)
            for h in range(HG):
                pool.wait_ge(S["exp_a"], 4 * h + 4)
                g.tensor_tensor(enb[:, h], kf[:, h], enb[:, h], ALU.mult)
                g.tensor_tensor(lf[:, h], kf[:, h], lf[:, h], ALU.mult)
                pool.wait_ge(S["qs_a"], h + 1)
                g.tensor_tensor(qs[:, h], qs[:, h], eb[:, h], ALU.mult).then_inc(S["dec_p"], 1)
            for n in range(2 * NT):
                b, t = n // NT, n % NT
                pool.wait_ge(S["gate_a"], n + 1)
                gv = gate[:, t, b * 256:(b + 1) * 256].rearrange("p (h v) -> p h v", v=DV)
                g.tensor_tensor(gv, gv, norm_row[:].unsqueeze(1).broadcast_to([P, 2, DV]), ALU.mult)\
                    .then_inc(S["gate_p"], 1)
            for h in range(HG):
                pool.wait_ge(S["sc_a"], h + 1)
                sv = sT[:, h].rearrange("p (t c) -> p t c", c=P)
                link(g.affine_select(out=sv, in_=sv, compare_op=ALU.is_ge, fill=0.0, base=0,
                                     pattern=[[0, NT], [1, P]], channel_multiplier=-1))
                g.memset(sv[0:CHUNK, :, CHUNK:P], 0.0).then_inc(S["sc_p"], 1)
            pool.wait_ge(S["units"], made(f"sg{NT - 1}"))
            g.memset(xg[:], 0.0).then_inc(S["xg_clear"], 1)
            pool.wait_ge(S["xg_clear"], 1)
            last_token = pool.to_reg(SEQ - 1)
            last_row = pool.to_reg(SEQ * TK - 1)

            def gather(i, u):
                pool.wait_ge(S["idx_v"], i + 1)
                if not isinstance(i, int) or i >= SLOTS:
                    pool.wait_ge(S["xt_m"], i + (1 - SLOTS))
                pool.sem_inc(S["turn_p"], 1)
                pool.indirect_dma_start(out=xg[0:CAP, u, :], out_offset=None, in_=h_rows,
                                        in_offset=bass.IndirectOffsetOnAxis(ap=idx_g[0:CAP, u:u + 1], axis=0),
                                        bounds_check=last_token, oob_is_err=False).then_inc(X_GA[u], 16)

            def scatter(i, u):
                pool.wait_ge(S["y_a"], i + 1)
                pool.wait_ge(S["y_v"], i + 1)
                pool.sem_inc(S["turn_p"], 1)
                pool.indirect_dma_start(out=y_rows, out_offset=bass.IndirectOffsetOnAxis(ap=idx_s[0:CAP, u:u + 1], axis=0),
                                        in_=y_sb[0:CAP, u, :], in_offset=None,
                                        bounds_check=last_row, oob_is_err=False).then_inc(Y_ST[u], 16)

            def group(i0, first=False, last=False):
                for u in range(SLOTS):
                    if not (last and u >= 1):
                        gather(i0 + (u + 3), (u + 3) % SLOTS)
                    if not (first and u == 0):
                        scatter(i0 + (u - 1), (u + 3) % SLOTS)

            pool.wait_ge(S["st_h"], 16 * NT)
            gather(0, 0)
            gather(1, 1)
            gather(2, 2)
            pool.wait_ge(S["nch_ready"], 1)
            n_mid = pool.value_load(n_int[0:1, 0:1], min_val=GROUPS - 2, max_val=GROUPS * MAXC - 2)
            group(0, first=True)
            group(SLOTS)
            with pool.Fori(2, n_mid + 1) as n:
                group(pool.snap(n * SLOTS))
            i0 = pool.snap(n_mid * SLOTS + SLOTS)
            group(i0, last=True)
            scatter(i0 + 3, 3)
            pool.wait_ge(S["ld_ln2"], 32)

            def pair_sums(t):
                for j in range(2):
                    pool.wait_ge(S[f"y_ld{t % 2}{j}"], 16 * (t // 2 + 1))
                    g.tensor_tensor(y_in[:, t % 2, 2 * j], y_in[:, t % 2, 2 * j], y_in[:, t % 2, 2 * j + 1], ALU.add)\
                        .then_inc(S["pair_p"], 1)

            pair_sums(0)
            for t in range(NT - 1):
                pair_sums(t + 1)
                pool.wait_ge(S["ln2r_a"], t + 1)
                g.tensor_tensor(acc[:, t], acc[:, t], ln_b, ALU.add).then_inc(S["fin_p"], 1)

        @block.scalar
        def _(act):
            a = nc.scalar

            def copy(o, i):
                return a.activation(o, i, ACT.Copy)

            for t in range(NT):
                act.wait_ge(S["units"], made(f"xt{t}1"))
                copy(xT[:, 4:8, t * P:(t + 1) * P], bank(f"xt{t}1").rearrange("p (k c) -> p k c", c=P)).then_inc(S["xT_a"], 1)
            for n, name in enumerate(("cq0", "cq1", "ckv")):
                act.wait_ge(S["units"], made(name))
                copy(cqT[:, n] if n < 2 else ckT, bank(name))
                a.activation(sq[:, n], bank(name), ACT.Square).then_inc(S["lat_a"], 1)
            act.wait_ge(S["units"], made("kidx"))
            copy(kxT, bank("kidx")).then_inc(S["kx_a"], 1)
            act.wait_ge(S["lb_v"], 1)
            a.activation(lbl[:], lbl[:], ACT.Exp).then_inc(S["lb_a"], 1)
            act.wait_ge(S["units"], made("hf0"))
            a.activation(lf[:, 0], bank("hf0"), ACT.Sigmoid).then_inc(S["sig_a"], 1)
            act.wait_ge(S["consts"], 2)
            a.activation(dist[:], dist[:], ACT.Abs)
            act.wait_ge(S["units"], made("ss_cq"))
            a.activation(rt[:, 0], bank("ss_cq"), ACT.Sqrt, bias=eps_t[:, 0:1], scale=1.0 / QR).then_inc(S["sqrt_a"], 1)
            act.wait_ge(S["units"], made("ss_ckv"))
            a.activation(rt[:, 1], bank("ss_ckv"), ACT.Sqrt, bias=eps_t[:, 0:1], scale=1.0 / KVR).then_inc(S["sqrt_a"], 1)
            act.wait_ge(S["xc_v"], 1)
            a.activation(sqk, kxT, ACT.Square).then_inc(S["sqk_a"], 1)
            act.wait_ge(S["units"], made("var_k"))
            a.activation(rt[:, 2], bank("var_k"), ACT.Sqrt, bias=eps_t[:, 1:2], scale=1.0 / P).then_inc(S["sqrt_a"], 1)
            for h in range(1, HG):
                act.wait_ge(S["units"], made(f"hf{h}"))
                a.activation(lf[:, h], bank(f"hf{h}"), ACT.Sigmoid).then_inc(S["sig_a"], 1)
            for m in range(2):
                act.wait_ge(S["units"], made(f"qidx{m}"))
                copy(qiT[:, m], bank(f"qidx{m}")).then_inc(S["qidx_a"], 1)
            for h in range(HG):
                act.wait_ge(S["f_v"], h + 1)
                a.activation(lf[:, h], lf[:, h], ACT.Ln).then_inc(S["lnf_a"], 1)

            def relus(t):
                for i in range(IH):
                    n = IH * (t - 1) + i
                    act.wait_ge(S["units"], made(f"lg{t}{i}"))
                    if n >= 2:
                        act.wait_ge(S["idxs_v"], n - 1)
                    a.activation(relu_t[:, n % 2, 0:(t + 1) * P], bank(f"lg{t}{i}")[:, 0:(t + 1) * P],
                                 ACT.Relu).then_inc(S["relu_a"], 1)

            relus(1)
            for m in range(4):
                act.wait_ge(S["units"], made(f"qu{m}"))
                a.activation(qT[:, m], bank(f"qu{m}"), ACT.Copy, scale=DH ** -0.5).then_inc(S["up_a"], 1)
            for m in range(4):
                act.wait_ge(S["units"], made(f"ku{m}"))
                copy(kT[:, m], bank(f"ku{m}")).then_inc(S["up_a"], 1)
            for t in range(NT):
                act.wait_ge(S["units"], made(f"vu{t}"))
                copy(v_at[:, t], bank(f"vu{t}")).then_inc(S["up_a"], 1)
            for h in range(HG):
                act.wait_ge(S["bsum_v"], 2 * h + 2)
                a.activation(eb[:, h], lf[:, h], ACT.Exp).then_inc(S["exp_a"], 1)
                a.activation(enb[:, h], lf[:, h], ACT.Exp, scale=-1.0).then_inc(S["exp_a"], 1)
                a.activation(dec[:, h], lf[:, h].rearrange("p (c s) -> p c s", s=CHUNK)[:, :, CHUNK - 1], ACT.Exp)\
                    .then_inc(S["exp_a"], 1)
                act.wait_ge(S["exp_a"], 4 * h + 3)
                a.activation(lf[:, h], qs[:, h], ACT.Exp).then_inc(S["exp_a"], 1)
            relus(2)
            for h in range(HG):
                act.wait_ge(S["units"], made(f"hq{h}"))
                a.activation(qs[:, h], bank(f"hq{h}"), ACT.Silu).then_inc(S["qs_a"], 1)
            relus(3)
            for b in range(2):
                for t in range(NT):
                    act.wait_ge(S["units"], made(f"hi{b}{t}"))
                    copy(v_hg[:, t, b * 256:(b + 1) * 256], bank(f"hi{b}{t}")[:, 0:256]).then_inc(S["vh_a"], 1)
            for b in range(2):
                for t in range(NT):
                    act.wait_ge(S["units"], made(f"hg{b}{t}"))
                    a.activation(gate[:, t, b * 256:(b + 1) * 256], bank(f"hg{b}{t}")[:, 0:256], ACT.Silu)\
                        .then_inc(S["gate_a"], 1)

            def rms_root(h):
                act.wait_ge(S["sq_a"], h + 1)
                a.activation(r_o[:, h], ss_o[:, h], ACT.Sqrt, bias=eps_t[:, 0:1], scale=1.0 / DV).then_inc(S["rsq_a"], 1)

            for h in range(HG + 1):
                if h < HG:
                    act.wait_ge(S["dec_p"], HG)
                    act.wait_ge(S["units"], made(f"kd{h}"))
                    copy(kdN[:, h], bank(f"kd{h}")).then_inc(S["kd_a"], 1)
                    act.wait_ge(S["units"], made(f"sc{h}"))
                    copy(sT[:, h], bank(f"sc{h}")).then_inc(S["sc_a"], 1)
                if h:
                    act.wait_ge(S["units"], made(f"o{h - 1}"))
                    copy(o_hg[:, h - 1], bank(f"o{h - 1}"))
                    a.activation(qs[:, h - 1], bank(f"o{h - 1}"), ACT.Square).then_inc(S["o_a"], 1)
                if h > 1:
                    rms_root(h - 2)
            rms_root(HG - 1)

            def probs(i):
                t, h = pairs[i]
                n = (t + 1) * P
                act.wait_ge(S["biasd_v"], 2 * i + 2)
                if i >= 2:
                    act.wait_ge(S["units"], made("PT%d%d" % pairs[i - 2]))
                a.activation(at_p[:, i % 2, 0:n], at_s[:, i % 2, 0:n], ACT.Exp, bias=nmax[:, i:i + 1],
                             accum_out=rsum[:, i:i + 1]).then_inc(S["prob_a"], 1)

            def probs_t(i):
                t, h = pairs[i]
                n = (t + 1) * P
                act.wait_ge(S["units"], made("PT%d%d" % (t, h)))
                if i >= 2:
                    tt, hh = pairs[i - 2]
                    act.wait_ge(S["units"], made(f"PV{tt}{hh // 2}"))
                copy(at_pT[:, i % 2, 0:n], bank("PT%d%d" % (t, h))[:, 0:n]).then_inc(S["pT_a"], 1)

            def heads_out(i):
                t, h = pairs[i]
                name = f"PV{t}{h // 2}"
                act.wait_ge(S["units"], made(name))
                copy(oT[:, 4 + h // 2, t * P:(t + 1) * P], bank(name)[:, 0:P]).then_inc(S["pv_a"], 1)

            for i in range(len(pairs) + 3):
                if i < len(pairs):
                    probs(i)
                    t, h = pairs[i]
                    if t == 0 and h in MIX_AT:
                        n = MIX_AT.index(h)
                        act.wait_ge(S["units"], made(f"oaT{n}"))
                        copy(oT[:, n], bank(f"oaT{n}")).then_inc(S["oT_a"], 1)
                if 0 <= i - 2 < len(pairs):
                    probs_t(i - 2)
                if 0 <= i - 3 < len(pairs) and pairs[i - 3][1] % 2:
                    heads_out(i - 3)

            def rstd(ts):
                for t in ts:
                    act.wait_ge(S["lnv_v"], t + 1)
                    a.activation(rs[:, t:t + 1], mv[:, t, 1:2], ACT.Sqrt, bias=eps_t[:, 1:2]).then_inc(S["lns_a"], 1)

            def normed_rows(t):
                act.wait_ge(S["units"], made(f"hT{t}1"))
                copy(hT[:, 4:8, t * P:(t + 1) * P], bank(f"hT{t}1").rearrange("p (k c) -> p k c", c=P))\
                    .then_inc(S["hT_a"], 1)

            def router_scores(t):
                act.wait_ge(S["units"], made(f"rl{t}"))
                a.activation(R[0][:, t], bank(f"rl{t}")[:, 0:NE], ACT.Sigmoid).then_inc(S["rl_a"], 1)

            def shared_silu(t):
                act.wait_ge(S["units"], made(f"sg{t}"))
                if t >= 2:
                    act.wait_ge(S["sh_h"], t - 1)
                a.activation(silu_g[:, t % 2], bank(f"sg{t}")[:, 0:DE], ACT.Silu).then_inc(S["sh_si"], 1)

            def shared_t(t):
                act.wait_ge(S["units"], made(f"st{t}"))
                if t >= 2:
                    act.wait_ge(S["units"], made(f"sd{t - 2}1"))
                copy(heT[:, t % 2], bank(f"st{t}")[:, 0:DE]).then_inc(S["sh_t"], 1)

            rstd(range(NT - 1))
            normed_rows(0)
            normed_rows(1)
            rstd([NT - 1])
            normed_rows(2)
            router_scores(0)
            router_scores(1)
            normed_rows(3)
            router_scores(2)
            router_scores(3)
            for t in range(2):
                shared_silu(t)
            for t in range(NT):
                shared_t(t)
                if t + 2 < NT:
                    shared_silu(t + 2)

            act.wait_ge(S["nch_ready"], 1)
            n_mid = act.value_load(n_int[0:1, 0:1], min_val=GROUPS - 2, max_val=GROUPS * MAXC - 2)

            def rows_t(i, u, early):
                act.wait_ge(S["xt_m"], i + 1)
                if not early:
                    act.wait_ge(S["gu_m"], i - 1)
                copy(xgT[:, i2(u)].rearrange("p (b c) -> p b c", b=2), ps[:, 0:2, 0:KD // 2 * CAP]).then_inc(S["xt_e"], 1)

            def hidden_t(i, u, early):
                act.wait_ge(S["ht_m"], i + 1)
                if not early:
                    act.wait_ge(S["dn_m"], i - 1)
                copy(heT_x[:, i2(u)], ps[:, 4, 0:2 * CAP]).then_inc(S["ht_a"], 1)

            def silu(i, u, early):
                act.wait_ge(S["gu_m"], i + 1)
                if not early:
                    act.wait_ge(S["h_v"], i - 1)
                a.activation(silu_g[0:CAP, i2(u)], ps[0:CAP, 2 + i2(u), 0:DE], ACT.Silu).then_inc(S["si_a"], 1)

            def y_half(i, u, stored):
                act.wait_ge(S["dn_m"], i + 1)
                if stored is not None:
                    act.wait_ge(Y_ST[u], stored)
                copy(y_sb[0:CAP, u, 0:512], ps[0:CAP, 5, :]).then_inc(S["y_a"], 1)

            def group(i0, n, first=False, last=False):
                for u in range(SLOTS):
                    if not (last and u == SLOTS - 1):
                        rows_t(i0 + (u + 1), u + 1, first and u < 1)
                    if not (first and u == 0):
                        hidden_t(i0 + (u - 1), u + 3, first and u < 3)
                    silu(i0 + u, u, first and u < 2)
                    if not (first and u == 0):
                        y_half(i0 + (u - 1), (u + 3) % SLOTS, stored_before(u, n, first))

            rows_t(0, 0, True)
            group(0, 0, first=True)
            group(SLOTS, 1)
            with act.Fori(2, n_mid + 1) as n:
                group(act.snap(n * SLOTS), n)
            i0 = act.snap(n_mid * SLOTS + SLOTS)
            n_last = act.snap(n_mid + 1)
            group(i0, n_last, last=True)
            hidden_t(i0 + 3, 3, False)
            y_half(i0 + 3, 3, n_last * 16)
            for t in range(NT):
                act.wait_ge(S["ln2v_v"], t + 1)
                a.activation(rs[:, t:t + 1], mv[:, t, 1:2], ACT.Sqrt, bias=eps_t[:, 1:2]).then_inc(S["ln2s_a"], 1)
                if t < NT - 1:
                    act.wait_ge(S["ln2n_v"], t + 1)
                    a.activation(acc[:, t], acc[:, t], ACT.Copy, scale=rs[:, t:t + 1]).then_inc(S["ln2r_a"], 1)

        @block.vector
        def _(dve):
            v = nc.vector
            link = linker(dve, "link_v")
            for t in range(NT):
                dve.wait_ge(S["units"], made(f"xt{t}0"))
                v.tensor_copy(xT[:, 0:4, t * P:(t + 1) * P], bank(f"xt{t}0").rearrange("p (k c) -> p k c", c=P))\
                    .then_inc(S["xT_v"], 1)
            dve.wait_ge(S["ld_small"], 144)
            link(v.tensor_tensor(lb[:], lbl[:, 0], lbl[:, 1], ALU.max))
            v.tensor_tensor(lbl[:], lbl[:], lb[:].unsqueeze(1).broadcast_to([P, 2, HG]), ALU.subtract)\
                .then_inc(S["lb_v"], 1)
            dve.wait_ge(S["lb_a"], 1)
            link(v.tensor_tensor(one_lb[:], lbl[:, 0], lbl[:, 1], ALU.add))
            link(v.reciprocal(one_lb[:], one_lb[:]))
            link(v.tensor_tensor(lb[:], lbl[:, 0], one_lb[:], ALU.mult))
            link(v.tensor_scalar(one_lb[:], lb[:], -1.0, 1.0, ALU.mult, ALU.add))
            dve.wait_ge(S["consts"], 2)
            dve.wait_ge(S["units"], made("widx"))
            v.tensor_scalar(w_i[:], bank("widx")[:, 0:NT * IH].rearrange("p (t i) -> p t i", i=IH),
                            IH ** -0.5, IDH ** -0.5, ALU.mult, ALU.mult).then_inc(S["wi_v"], 1)
            dve.wait_ge(S["units"], made("mean_k"))
            v.scalar_tensor_tensor(kxT, bank("mean_k"), -1.0 / P, kxT, ALU.mult, ALU.add).then_inc(S["xc_v"], 1)
            dve.wait_ge(S["sqrt_a"], 2)
            link(v.reciprocal(rt[:, 0:2], rt[:, 0:2]))
            for m in range(2):
                v.scalar_tensor_tensor(cqT[:, m], cqT[:, m], gq[:, m:m + 1], rt[:, 0], ALU.mult, ALU.mult)\
                    .then_inc(S["norm_v"], 1)
            v.scalar_tensor_tensor(ckT, ckT, gkv[:, 0:1], rt[:, 1], ALU.mult, ALU.mult).then_inc(S["norm_v"], 1)
            dve.wait_ge(S["sqrt_a"], 3)
            link(v.reciprocal(rt[:, 2], rt[:, 2]))
            link(v.scalar_tensor_tensor(kxT, kxT, gk[:, 0:1], rt[:, 2], ALU.mult, ALU.mult))
            v.tensor_scalar(kxT, kxT, bk[:, 0:1], None, ALU.add).then_inc(S["kn_v"], 1)
            for h in range(HG):
                dve.wait_ge(S["sig_a"], h + 1)
                link(v.tensor_scalar(lf[:, h], lf[:, h], one_lb[:, h:h + 1], lb[:, h:h + 1], ALU.mult, ALU.add))
                v.tensor_scalar(kf[:, h], lf[:, h], -1.0, 1.0, ALU.mult, ALU.add).then_inc(S["f_v"], 1)
            for h in range(HG):
                dve.wait_ge(S["lnf_a"], h + 1)
                v.tensor_tensor_scan(lf[:, h], keep[:], lf[:, h], 0.0, ALU.mult, ALU.add).then_inc(S["bsum_v"], 1)
                dve.wait_ge(S["bsum_v"], 2 * h + 1)
                bv = lf[:, h].rearrange("p (c s) -> p c s", s=CHUNK)
                v.tensor_tensor(qs[:, h].rearrange("p (c s) -> p c s", s=CHUNK),
                                bv[:, :, CHUNK - 1:CHUNK].broadcast_to([P, NCH, CHUNK]), bv, ALU.subtract)\
                    .then_inc(S["bsum_v"], 1)

            link(v.memset(sel_mask[0][:], 0.0))
            v.memset(sel_mask[0][0:CHUNK, CHUNK:P], -NEG).then_inc(S["mask_v"], 1)
            for t in range(1, NT):
                n = (t + 1) * P
                for i in range(IH):
                    u = IH * (t - 1) + i
                    dve.wait_ge(S["relu_a"], u + 1)
                    if i == 0:
                        ins = v.tensor_scalar(score[:, 0:n], relu_t[:, u % 2, 0:n], w_i[:, t, 0:1], None, ALU.mult)
                    else:
                        ins = v.scalar_tensor_tensor(score[:, 0:n], relu_t[:, u % 2, 0:n], w_i[:, t, i:i + 1],
                                                     score[:, 0:n], ALU.mult, ALU.add)
                    ins.then_inc(S["idxs_v"], 1)
                    dve.wait_ge(S["idxs_v"], u + 1)
                link(v.memset(score[0:CHUNK, n - CHUNK:n], -3e38))
                cur = score
                for r in range(TOPK // 8):
                    link(v.max(top8[:], cur[:, 0:n]))
                    if r < TOPK // 8 - 1:
                        link(v.match_replace(work[:, 0:n], top8[:], cur[:, 0:n], -3.2e38))
                        cur = work
                link(v.tensor_scalar(m_eq[:, 0:n], score[:, 0:n], top8[:, 7:8], None, ALU.is_equal))
                link(v.tensor_tensor_scan(m_cum[:, 0:n], ones[:, 0:1].broadcast_to([P, n]), m_eq[:, 0:n], 0.0, ALU.mult, ALU.add))
                link(v.tensor_scalar(work[:, 0:n], score[:, 0:n], top8[:, 7:8], None, ALU.is_gt, ALU.add,
                                     accum_out=cnt[:, 0:1]))
                link(v.tensor_scalar(cnt[:, 1:2], cnt[:, 0:1], -1.0, float(TOPK), ALU.mult, ALU.add))
                link(v.scalar_tensor_tensor(m_eq[:, 0:n], m_cum[:, 0:n], cnt[:, 1:2], m_eq[:, 0:n], ALU.is_le, ALU.mult))
                link(v.tensor_tensor(work[:, 0:n], work[:, 0:n], m_eq[:, 0:n], ALU.add))
                v.tensor_scalar(sel_mask[t], work[:, 0:n], -1.0, NEG, ALU.add, ALU.mult).then_inc(S["mask_v"], 1)

            def squares(h):
                dve.wait_ge(S["o_a"], h + 1)
                v.tensor_reduce(ss_o[:, h], qs[:, h].rearrange("p (t v) -> p t v", v=DV), AX.X, ALU.add)\
                    .then_inc(S["sq_a"], 1)

            def mixer_a(h):
                dve.wait_ge(S["gate_p"], 2 * NT)
                dve.wait_ge(S["rsq_a"], h + 1)
                link(v.reciprocal(r_o[:, h], r_o[:, h]))
                ov = o_hg[:, h].rearrange("p (t v) -> p t v", v=DV)
                link(v.tensor_tensor(ov, ov, r_o[:, h].unsqueeze(2).broadcast_to([P, NT, DV]), ALU.mult))
                v.tensor_tensor(mix_a[:, h].rearrange("p (t v) -> p t v", v=DV), ov,
                                gate[:, :, h * DV:(h + 1) * DV], ALU.mult).then_inc(S["oa_v"], 1)

            for h in range(HG):
                for c in range(NCH - 1):
                    if c == 0:
                        dve.wait_ge(S["units"], made(f"dsb{h}"))
                        if h >= 2:
                            dve.wait_ge(S["units"], made(f"o{h - 2}"))
                    d = bank(f"ds{'ab'[c % 2]}{h}")[:, (c // 2) * DV:(c // 2 + 1) * DV]
                    if c == 0:
                        ins = v.tensor_copy(states[:, h % 2, 1], d)
                    else:
                        ins = v.scalar_tensor_tensor(states[:, h % 2, c + 1], states[:, h % 2, c],
                                                     dec[:, h, c:c + 1], d, ALU.mult, ALU.add)
                    ins.then_inc(S["st_v"], 1)
                    dve.wait_ge(S["st_v"], 7 * h + c + 1)
                if h > 1:
                    mixer_a(h - 2)
                if h:
                    squares(h - 1)
            squares(HG - 1)
            def scores(i):
                t, h = pairs[i]
                n = (t + 1) * P
                slope = 2.0 ** (-8.0 * (h + 1) / AH)
                link(v.scalar_tensor_tensor(at_bias[:, i % 2, 0:n], dist[:, SEQ - P - t * P:SEQ], -slope,
                                            sel_mask[t], ALU.mult, ALU.add))
                dve.wait_ge(S["units"], made("S%d%d" % (t, h)))
                if i >= 2:
                    dve.wait_ge(S["prob_a"], i - 1)
                v.tensor_tensor(at_s[:, i % 2, 0:n], bank("S%d%d" % (t, h))[:, 0:n], at_bias[:, i % 2, 0:n], ALU.add)\
                    .then_inc(S["biasd_v"], 1)
                dve.wait_ge(S["biasd_v"], 2 * i + 1)
                v.tensor_reduce(nmax[:, i:i + 1], at_s[:, i % 2, 0:n], AX.X, ALU.max, negate=True)\
                    .then_inc(S["biasd_v"], 1)

            def normed(i):
                t, h = pairs[i]
                n = (t + 1) * P
                dve.wait_ge(S["prob_a"], i + 1)
                link(v.reciprocal(rinv[:, i:i + 1], rsum[:, i:i + 1]))
                v.tensor_scalar(at_p[:, i % 2, 0:n], at_p[:, i % 2, 0:n], rinv[:, i:i + 1], None, ALU.mult)\
                    .then_inc(S["norm2_v"], 1)

            def residual(t, half):
                dve.wait_ge(S["units"], made(f"out{t}{half}"))
                dve.wait_ge(S["ld_xr"], 16)
                xv = acc[:, t, half * 512:(half + 1) * 512]
                v.scalar_tensor_tensor(xv, xv, ALPHA, bank(f"out{t}{half}"), ALU.mult, ALU.add)\
                    .then_inc(S["res_v"], 1)

            def row_stats(t):
                dve.wait_ge(S["res_v"], 2 * t + 2)
                link(v.bn_stats(stats[:, 0], acc[:, t, 0:512]))
                link(v.bn_stats(stats[:, 1], acc[:, t, 512:1024]))
                v.bn_aggr(mv[:, t], stats[:]).then_inc(S["lnv_v"], 1)
                dve.wait_ge(S["lnv_v"], t + 1)

            def normalise(ts):
                dve.wait_ge(S["ld_ln"], 32)
                for t in ts:
                    link(v.scalar_tensor_tensor(acc[:, t], acc[:, t], mv[:, t, 0:1], ln_g, ALU.subtract, ALU.mult))
                    dve.wait_ge(S["lns_a"], t + 1)
                    link(v.reciprocal(rs[:, t:t + 1], rs[:, t:t + 1]))
                    v.scalar_tensor_tensor(acc[:, t], acc[:, t], rs[:, t:t + 1], ln_b, ALU.mult, ALU.add)\
                        .then_inc(S["lnn_v"], 1)

            for i in range(len(pairs) + 1):
                if i < len(pairs):
                    scores(i)
                    t, h = pairs[i]
                    if i in (1, 2):
                        mixer_a(HG - 3 + i)
                    if t and h in OUT_AT:
                        residual(t - 1, OUT_AT.index(h))
                if i:
                    normed(i - 1)
            for t in range(NT - 1):
                row_stats(t)
            normalise(range(NT - 1))

            def hidden_rows(ts):
                for t in ts:
                    dve.wait_ge(S["units"], made(f"hT{t}0"))
                    v.tensor_copy(hT[:, 0:4, t * P:(t + 1) * P], bank(f"hT{t}0").rearrange("p (k c) -> p k c", c=P))\
                        .then_inc(S["hT_v"], 1)

            for half in range(2):
                residual(NT - 1, half)
            hidden_rows([0])
            row_stats(NT - 1)
            hidden_rows([1])
            normalise([NT - 1])
            hidden_rows([2, 3])

            def shared_h(t):
                dve.wait_ge(S["sh_si"], t + 1)
                if t >= 2:
                    dve.wait_ge(S["units"], made(f"st{t - 2}"))
                v.tensor_tensor(h_e[:, t % 2], silu_g[:, t % 2], bank(f"sg{t}")[:, DE:2 * DE], ALU.mult)\
                    .then_inc(S["sh_h"], 1)

            def shared_y(t):
                for half in range(2):
                    dve.wait_ge(S["units"], made(f"sd{t}{half}"))
                    av = acc[:, t, half * 512:(half + 1) * 512]
                    v.scalar_tensor_tensor(av, av, ALPHA, bank(f"sd{t}{half}"), ALU.mult, ALU.add)\
                        .then_inc(S["sh_y"], 1)


            def per_tile(r, n=NE):
                return r.unsqueeze(2).broadcast_to([P, NT, n])

            def column(c):
                return meta[:, :, :, c].rearrange("p e t -> p t e")

            link(v.tensor_scalar(s4[:], tok_id[:], tok_id[:, 0:1], None, ALU.subtract))
            link(v.tensor_scalar(column(0), per_tile(s4[:]), -BIG, None, ALU.add))
            link(v.tensor_scalar(column(3), per_tile(s4[:]), float(TK), -BIG, ALU.mult, ALU.add))
            link(v.memset(column(2), 0.0))
            link(v.tensor_copy(column(1), tok_id[:, 0:1].unsqueeze(1).broadcast_to([P, NT, NE])))
            link(v.tensor_scalar(column(4), tok_id[:, 0:1].unsqueeze(1).broadcast_to([P, NT, NE]), float(TK), None,
                                 ALU.mult))
            dve.wait_ge(S["rl_a"], NT)

            def groups_of(r):
                return r.rearrange("p t (g e) -> p (t g) e", e=PER)

            def per_group(r):
                return r[:].unsqueeze(2).broadcast_to([P, NT * NG, PER])

            def flat(r):
                return r.rearrange("p t e -> p (t e)")

            link(v.tensor_tensor(R[1], R[0], bias_row[:].unsqueeze(1).broadcast_to([P, NT, NE]), ALU.add))
            link(v.tensor_reduce(g1[:], groups_of(R[1]), AX.X, ALU.max))
            link(v.tensor_tensor(groups_of(R[2]), groups_of(R[1]), per_group(g1), ALU.is_equal))
            link(v.tensor_reduce(g2[:], groups_of(R[2]), AX.X, ALU.add))
            link(v.scalar_tensor_tensor(flat(R[3]), flat(R[2]), -NEG, flat(R[1]), ALU.mult, ALU.add))
            link(v.tensor_reduce(g3[:], groups_of(R[3]), AX.X, ALU.max))
            link(v.tensor_scalar(g2[:], g2[:], 2.0, None, ALU.is_ge))
            link(v.tensor_scalar(g2[:], g2[:], -1.0, NEG, ALU.add, ALU.mult))
            link(v.tensor_tensor(g2[:], g2[:], g1[:], ALU.add))
            link(v.tensor_tensor(g3[:], g3[:], g2[:], ALU.max))
            link(v.tensor_tensor(g1[:], g1[:], g3[:], ALU.add))
            gj = g1[:].rearrange("p (t g) -> p t g", g=NG).unsqueeze(2).broadcast_to([P, NT, NG, NG])
            gi = g1[:].rearrange("p (t g) -> p t g", g=NG).unsqueeze(3).broadcast_to([P, NT, NG, NG])
            link(v.tensor_tensor(gr[:], gj, gi, ALU.is_gt))
            link(v.tensor_tensor(gr2, gj, gi, ALU.is_equal))
            link(v.tensor_tensor(gr2, gr2, before[:].unsqueeze(1).broadcast_to([P, NT, NG, NG]), ALU.mult))
            link(v.tensor_tensor(gr[:], gr[:], gr2, ALU.add))
            link(v.tensor_reduce(g2[:], gr[:].rearrange("p t i j -> p (t i) j"), AX.X, ALU.add))
            link(v.tensor_scalar(g2[:], g2[:], float(TG), None, ALU.is_lt))
            link(v.tensor_scalar(g2[:], g2[:], -1.0, NEG, ALU.add, ALU.mult))
            link(v.tensor_tensor(groups_of(R[3]), groups_of(R[1]), per_group(g2), ALU.add))
            for t in range(NT):
                link(v.max(t8[:, t], R[3][:, t]))
            eighth = t8[:, :, 7:8].broadcast_to([P, NT, NE])
            link(v.tensor_tensor(R[4], R[3], eighth, ALU.is_gt))
            link(v.tensor_tensor(R[5], R[3], eighth, ALU.is_equal))
            link(v.tensor_reduce(s4[:], R[4], AX.X, ALU.add))
            link(v.tensor_scalar(s4[:], s4[:], -1.0, float(TK), ALU.mult, ALU.add))
            link(v.tensor_tensor_scan(flat(R[6]), keep[:, 0:NT * NE], flat(R[5]), 0.0, ALU.mult, ALU.add))
            link(v.tensor_tensor(R[6], R[6], per_tile(s4[:]), ALU.is_le))
            link(v.tensor_tensor(R[5], R[5], R[6], ALU.mult))
            v.tensor_tensor(R[4], R[4], R[5], ALU.add).then_inc(S["ro_sel"], 1)
            dve.wait_ge(S["ro_sel"], 1)
            shared_h(0)
            link(v.tensor_tensor(R[5], R[0], R[4], ALU.mult))
            link(v.tensor_reduce(s5[:], R[5], AX.X, ALU.add))
            link(v.reciprocal(s5[:], s5[:]))
            link(v.tensor_tensor(R[5], R[5], per_tile(s5[:]), ALU.mult))

            link(v.tensor_scalar(R[5], R[5], ROUTED_SCALE, None, ALU.mult))
            link(v.tensor_copy(column(6), R[5]))
            link(v.tensor_tensor_scan(flat(R[6]), keep[:, 0:NT * NE], flat(R[4]), 0.0, ALU.mult, ALU.add))
            link(v.tensor_scalar(column(5), R[6], -1.0, None, ALU.add))
            link(v.tensor_tensor(R[5], R[5], column(6), ALU.subtract))
            link(v.tensor_copy(column(7), R[5]))
            link(v.tensor_tensor(column(8), R[5], column(7), ALU.subtract))
            shared_h(1)
            dve.wait_ge(S["pos_m"], 1)
            link(v.scalar_tensor_tensor(R[6], ps[:, 7, 0:NT * NE].rearrange("p (t e) -> p t e", e=NE), 1.0,
                                        R[4], ALU.add, ALU.mult))
            for c in range(MAXC):
                ins = v.tensor_scalar(pos_x[:, c * NE:(c + 1) * NE, :].rearrange("p e t -> p t e"), R[6],
                                      -1.0 - CAP * c, None, ALU.add)
            link(ins)
            def placed(i, u, early=False):
                if not early:
                    dve.wait_ge(S["idxm"], i - 1)
                at_i = pos_x[:, i, :] if isinstance(i, int) else \
                    pos_x[:, bass.ds(i, 1), :].rearrange("p o t -> p (o t)")
                v.tensor_tensor(place[:, i2(u)], slot_id[:, 0:CAP].unsqueeze(1).broadcast_to([P, NT, CAP]),
                                at_i.unsqueeze(2).broadcast_to([P, NT, CAP]), ALU.is_equal).then_inc(S["place_v"], 1)

            def indices(i, u):
                dve.wait_ge(S["idxm"], i + 1)
                if not isinstance(i, int) or i >= SLOTS:
                    dve.wait_ge(S["xt_m"], i + (1 - SLOTS))
                    dve.wait_ge(S["h_v"], i + (1 - SLOTS))
                v.tensor_reduce(slot_v[0:CAP, u], ps[0:CAP, 7, 0:META].rearrange("p (j c) -> p j c", c=3), AX.X, ALU.add)\
                    .then_inc(S["slot_r"], 1)
                dve.wait_ge(S["slot_r"], i + 1)
                v.tensor_scalar(idx_g[0:CAP, u:u + 1], slot_v[0:CAP, u, 0:1], BIG, None, ALU.add).then_inc(S["idx_v"], 1)

            def hidden(i, u, n, early):
                dve.wait_ge(S["idx_v"], i + 1)
                if not isinstance(n, int) or n:
                    dve.wait_ge(Y_ST[u], n * 16)
                v.tensor_scalar(idx_s[0:CAP, u:u + 1], slot_v[0:CAP, u, 1:2], BIG, None, ALU.add)
                dve.wait_ge(S["si_a"], i + 1)
                if not early:
                    dve.wait_ge(S["ht_m"], i - 1)
                v.scalar_tensor_tensor(h_e[0:CAP, i2(u)], ps[0:CAP, 2 + i2(u), DE:2 * DE], slot_v[0:CAP, u, 2:3],
                                       silu_g[0:CAP, i2(u)], ALU.mult, ALU.mult).then_inc(S["h_v"], 1)

            def y_half(i, u, stored):
                dve.wait_ge(S["dn_m"], i + 1)
                if stored is not None:
                    dve.wait_ge(Y_ST[u], stored)
                v.tensor_copy(y_sb[0:CAP, u, 512:1024], ps[0:CAP, 6, :]).then_inc(S["y_v"], 1)

            def group(i0, n, first=False, last=False):
                for u in range(SLOTS):
                    if not (last and u >= 1):
                        indices(i0 + (u + 3), (u + 3) % SLOTS)
                    if not last:
                        placed(i0 + (u + 4), u)
                    hidden(i0 + u, u, n, first and u < 2)
                    if not (first and u == 0):
                        y_half(i0 + (u - 1), (u + 3) % SLOTS, stored_before(u, n, first))

            link(v.tensor_reduce(n_max[:, 0:1], ps[:, 7, NT * NE:(NT + 1) * NE], AX.X, ALU.max))
            placed(0, 0, True)
            placed(1, 1, True)
            link(v.tensor_scalar(n_max[:, 1:2], n_max[:, 0:1], float(CAP), None, ALU.is_gt))
            for c in range(2, MAXC):
                link(v.scalar_tensor_tensor(n_max[:, c:c + 1], n_max[:, 0:1], float(CAP * c), n_max[:, c - 1:c],
                                            ALU.is_gt, ALU.add))
            v.tensor_scalar(n_int[:], n_max[:, MAXC - 1:MAXC], float(GROUPS), float(GROUPS - 2), ALU.mult, ALU.add)\
                .then_inc(S["nch_ready"], 1)
            shared_h(2)
            dve.wait_ge(S["st_h"], 16 * NT)
            shared_y(0)
            indices(0, 0)
            placed(2, 2)
            shared_h(3)
            shared_y(1)
            indices(1, 1)
            placed(3, 3)
            shared_y(2)
            indices(2, 2)
            shared_y(3)
            dve.wait_ge(S["nch_ready"], 1)
            n_mid = dve.value_load(n_int[0:1, 0:1], min_val=GROUPS - 2, max_val=GROUPS * MAXC - 2)

            group(0, 0, first=True)
            group(SLOTS, 1)
            with dve.Fori(2, n_mid + 1) as n:
                group(dve.snap(n * SLOTS), n)
            i0 = dve.snap(n_mid * SLOTS + SLOTS)
            n_last = dve.snap(n_mid + 1)
            group(i0, n_last, last=True)
            y_half(i0 + 3, 3, n_last * 16)
            dve.wait_ge(S["ld_ln2"], 32)
            for t in range(NT):
                for n, k in enumerate(FIN_ORDER):
                    if k in (0, 2):
                        dve.wait_ge(S["pair_p"], 2 * t + k // 2 + 1)
                    elif k % 2 == 0:
                        dve.wait_ge(S[f"y_ld{t % 2}{k // 2}"], 16 * (t // 2 + 1))
                    v.tensor_tensor(acc[:, t], acc[:, t], y_in[:, t % 2, k], ALU.add).then_inc(S["fin_v"], 1)
                    dve.wait_ge(S["fin_v"], len(FIN_ORDER) * t + n + 1)
                link(v.bn_stats(stats[:, 0], acc[:, t, 0:512]))
                link(v.bn_stats(stats[:, 1], acc[:, t, 512:1024]))
                v.bn_aggr(mv[:, t], stats[:]).then_inc(S["ln2v_v"], 1)
                dve.wait_ge(S["ln2v_v"], t + 1)
                link(v.scalar_tensor_tensor(acc[:, t], acc[:, t], mv[:, t, 0:1], ln_g, ALU.subtract, ALU.mult))
                dve.wait_ge(S["ln2s_a"], t + 1)
                v.reciprocal(rs[:, t:t + 1], rs[:, t:t + 1]).then_inc(S["ln2n_v"], 1)
                dve.wait_ge(S["ln2n_v"], t + 1)
            for half in range(2):
                cols = slice(half * 512, (half + 1) * 512)
                v.scalar_tensor_tensor(acc[:, NT - 1, cols], acc[:, NT - 1, cols], rs[:, NT - 1:NT], ln_b[:, cols],
                                       ALU.mult, ALU.add).then_inc(S["fin_h"], 1)

        @block.tensor
        def _(pe):
            m = nc.tensor.matmul
            pe.wait_ge(S["consts"], 1)
            for t in range(NT):
                pe.wait_ge(S[f"ld_x{t}"], 16)
                xv = x_nat[:, t].rearrange("p (c k) -> p k c", k=KD)
                for half in range(2):
                    o = pe_unit(pe, f"xt{t}{half}")
                    for k in range(4):
                        last = nc.tensor.transpose(o[:, k * P:(k + 1) * P], xv[:, 4 * half + k], ident[:])
                    last.then_inc(S["units"], 1)
            pe.wait_ge(S["xT_a"], NT)
            pe.wait_ge(S["xT_v"], NT)

            def project(name, w):
                o = pe_unit(pe, name)
                for k in range(KD):
                    last = m(o, w[:, k], xT[:, k], start=k == 0, stop=k == KD - 1)
                last.then_inc(S["units"], 1)

            pe.wait_ge(S["ld_cq0"], 16)
            project("cq0", w_lat[:, :, 0:128])
            pe.wait_ge(S["ld_lat"], 48)
            project("cq1", w_lat[:, :, 128:256])
            project("ckv", w_lat[:, :, 256:384])
            project("kidx", w_lat[:, :, 384:512])
            o = pe_unit(pe, "widx")
            for t in range(NT):
                for k in range(KD):
                    last = m(o[:, t * IH:(t + 1) * IH], xT[:, k, t * P:(t + 1) * P], w_lat[:, k, 512:516],
                             start=k == 0, stop=k == KD - 1)
            last.then_inc(S["units"], 1)

            def f_unit(h):
                if h % 2 == 0:
                    pe.wait_ge(S[f"ld_blk{h // 2}"], 16)
                project(f"hf{h}", w_blk[h // 2][:, :, (h % 2) * DK:(h % 2 + 1) * DK])

            def across(name, parts):
                o = pe_unit(pe, name)
                for i, part in enumerate(parts):
                    last = m(o, ones[:], part, start=i == 0, stop=i == len(parts) - 1)
                last.then_inc(S["units"], 1)

            f_unit(0)
            pe.wait_ge(S["consts"], 2)
            pe.wait_ge(S["lat_a"], 3)
            across("ss_cq", [sq[:, 0], sq[:, 1]])
            across("ss_ckv", [sq[:, 2]])
            pe.wait_ge(S["kx_a"], 1)
            across("mean_k", [kxT])
            f_unit(1)
            pe.wait_ge(S["sqk_a"], 1)
            across("var_k", [sqk])
            f_unit(2)

            def up(name, w, src, n):
                o = pe_unit(pe, name)
                for k in range(n):
                    last = m(o, w[k], src[k], start=k == 0, stop=k == n - 1)
                last.then_inc(S["units"], 1)

            pe.wait_ge(S["ld_up"], 48)
            pe.wait_ge(S["norm_v"], 3)
            up("qidx0", [wqi_up[:, k, 0:P] for k in range(2)], [cqT[:, 0], cqT[:, 1]], 2)
            f_unit(3)
            up("qidx1", [wqi_up[:, k, P:2 * P] for k in range(2)], [cqT[:, 0], cqT[:, 1]], 2)

            def logits_of(t):
                for i in range(IH):
                    o = pe_unit(pe, f"lg{t}{i}")
                    lo = IDH * (i % 2)
                    m(o[:, 0:(t + 1) * P], qiT[lo:lo + IDH, i // 2, t * P:(t + 1) * P],
                      kxT[lo:lo + IDH, 0:(t + 1) * P], start=True, stop=True).then_inc(S["units"], 1)

            pe.wait_ge(S["qidx_a"], 2)
            pe.wait_ge(S["kn_v"], 1)
            logits_of(1)
            for j in range(4):
                up(f"qu{j}", [wq_up[:, k, j * P:(j + 1) * P] for k in range(2)], [cqT[:, 0], cqT[:, 1]], 2)
            for j in range(4):
                up(f"ku{j}", [wkv_up[:, j * P:(j + 1) * P]], [ckT], 1)
            for t in range(NT):
                up(f"vu{t}", [ckT[:, t * P:(t + 1) * P]], [wkv_up[:, AW:2 * AW]], 1)
            for h in range(HG):
                if h % 2 == 0:
                    pe.wait_ge(S[f"ld_blk{h // 2}"], 32)
                project(f"hq{h}", w_blk[h // 2][:, :, (h % 2) * DK:(h % 2 + 1) * DK])
                if h == 1:
                    logits_of(2)
            logits_of(3)
            for name, done in (("hi", 48), ("hg", 64)):
                for b in range(2):
                    pe.wait_ge(S[f"ld_blk{b}"], done)
                    for t in range(NT):
                        o = pe_unit(pe, f"{name}{b}{t}")
                        for k in range(KD):
                            last = m(o[:, 0:256], xT[:, k, t * P:(t + 1) * P], w_blk[b][:, k],
                                     start=k == 0, stop=k == KD - 1)
                        last.then_inc(S["units"], 1)

            for h in range(HG + 1):
                if h < HG:
                    pe.wait_ge(S["dec_p"], h + 1)
                    o = pe_unit(pe, f"kd{h}")
                    for t in range(NT):
                        last = nc.tensor.transpose(o[:, t * P:(t + 1) * P], lf[:, h, t * P:(t + 1) * P], ident[:])
                    last.then_inc(S["units"], 1)
                    o = pe_unit(pe, f"sc{h}")
                    for t in range(NT):
                        last = m(o[:, t * P:(t + 1) * P], enb[:, h, t * P:(t + 1) * P], qs[:, h, t * P:(t + 1) * P],
                                 start=True, stop=True)
                    last.then_inc(S["units"], 1)
                    pe.wait_ge(S["kd_a"], h + 1)
                    pe.wait_ge(S["vh_a"], 2 * NT)
                    for odd in range(2):
                        o = pe_unit(pe, f"ds{'ab'[odd]}{h}")
                        lo = CHUNK * odd
                        for t in range(NT - odd):
                            last = m(o[:, t * DV:(t + 1) * DV], kdN[lo:lo + CHUNK, h, t * P:(t + 1) * P],
                                     v_hg[lo:lo + CHUNK, t, h * DV:(h + 1) * DV], start=True, stop=True)
                        last.then_inc(S["units"], 1)
                if h:
                    g = h - 1
                    pe.wait_ge(S["sc_p"], g + 1)
                    pe.wait_ge(S["st_v"], 7 * g + 7)
                    o = pe_unit(pe, f"o{g}")
                    for t in range(NT):
                        last = m(o[:, t * DV:(t + 1) * DV], sT[:, g, t * P:(t + 1) * P],
                                 v_hg[:, t, g * DV:(g + 1) * DV], start=True, stop=False, skip_group_check=True)
                        for c in (2 * t, 2 * t + 1):
                            if c:
                                lo = CHUNK * (c % 2)
                                last = m(o[lo:lo + CHUNK, t * DV:(t + 1) * DV], qs[:, g, c * CHUNK:(c + 1) * CHUNK],
                                         states[:, g % 2, c], start=False, stop=True, skip_group_check=True)
                    last.then_inc(S["units"], 1)

            def scores(i):
                t, h = pairs[i]
                if i == 0:
                    pe.wait_ge(S["up_a"], 12)
                o = pe_unit(pe, "S%d%d" % (t, h))
                lo = DH * (h % 2)
                m(o[:, 0:(t + 1) * P], qT[lo:lo + DH, h // 2, t * P:(t + 1) * P], kT[lo:lo + DH, h // 2, 0:(t + 1) * P],
                  start=True, stop=True).then_inc(S["units"], 1)

            def probs_t(i):
                t, h = pairs[i]
                pe.wait_ge(S["norm2_v"], i + 1)
                o = pe_unit(pe, "PT%d%d" % (t, h))
                for j in range(t + 1):
                    last = nc.tensor.transpose(o[:, j * P:(j + 1) * P], at_p[:, i % 2, j * P:(j + 1) * P], ident[:])
                last.then_inc(S["units"], 1)

            def values(i):
                t, h = pairs[i]
                o = pe_unit(pe, f"PV{t}{h // 2}")
                pe.wait_ge(S["pT_a"], i + 1)
                for g in (0, 1):
                    for j in range(t + 1):
                        last = m(o[DH * g:DH * g + DH, 0:P], v_at[:, j, (h - 1 + g) * DH:(h + g) * DH],
                                 at_pT[:, g, j * P:(j + 1) * P], start=j == 0, stop=j == t)
                last.then_inc(S["units"], 1)

            def mix_out(t, half):
                pe.wait_ge(S["ld_wo"], 16)
                pe.wait_ge(S["pv_a"], 4 * (t + 1))
                pe.wait_ge(S["oT_a"], HG)
                o = pe_unit(pe, f"out{t}{half}")
                for k in range(KD):
                    last = m(o, oT[:, k, t * P:(t + 1) * P], w_o[:, k, half * 512:(half + 1) * 512],
                             start=k == 0, stop=k == KD - 1)
                last.then_inc(S["units"], 1)

            def mix_a_t(h):
                pe.wait_ge(S["oa_v"], h + 1)
                o = pe_unit(pe, f"oaT{h}")
                for t in range(NT):
                    last = nc.tensor.transpose(o[:, t * P:(t + 1) * P], mix_a[:, h, t * P:(t + 1) * P], ident[:])
                last.then_inc(S["units"], 1)

            for i in range(len(pairs) + 3):
                if i < len(pairs):
                    t, h = pairs[i]
                    scores(i)
                    if t and h in OUT_AT:
                        mix_out(t - 1, OUT_AT.index(h))
                    if t == 0 and h in MIX_AT:
                        mix_a_t(MIX_AT.index(h))
                if 0 <= i - 2 < len(pairs):
                    probs_t(i - 2)
                if 0 <= i - 3 < len(pairs) and pairs[i - 3][1] % 2:
                    values(i - 3)
            for half in range(2):
                mix_out(NT - 1, half)

            def normed_rows(t):
                pe.wait_ge(S["lnn_v"], t + 1)
                hv = acc[:, t].rearrange("p (c k) -> p k c", k=KD)
                for half in range(2):
                    o = pe_unit(pe, f"hT{t}{half}")
                    for k in range(4):
                        last = nc.tensor.transpose(o[:, k * P:(k + 1) * P], hv[:, 4 * half + k], ident[:])
                    last.then_inc(S["units"], 1)

            def router_logits(t):
                pe.wait_ge(S["hT_v"], t + 1)
                pe.wait_ge(S["hT_a"], t + 1)
                o = pe_unit(pe, f"rl{t}")
                for k in range(KD):
                    last = m(o[:, 0:NE], hT[:, k, t * P:(t + 1) * P], w_rt[:, k], start=k == 0, stop=k == KD - 1)
                last.then_inc(S["units"], 1)

            def transposed_hidden(o, h_row, n):
                hv = h_row.rearrange("p (c k) -> p k c", k=2)
                for k in range(2):
                    last = nc.tensor.transpose(o[:, k * n:(k + 1) * n], hv[:, k], ident[0:n, 0:n])
                return last

            def down(o, hid_t, w, half, n):
                for k in range(2):
                    last = m(o, hid_t[:, k * n:(k + 1) * n], w[:, k, half * 512:(half + 1) * 512],
                             start=k == 0, stop=k == 1)
                return last

            def shared_gate_up(t):
                o = pe_unit(pe, f"sg{t}")
                for k in range(KD):
                    last = m(o, hT[:, k, t * P:(t + 1) * P], ws_gu[:, :, k], start=k == 0, stop=k == KD - 1)
                last.then_inc(S["units"], 1)

            def shared_down(t):
                o = pe_unit(pe, f"st{t}")
                pe.wait_ge(S["sh_h"], t + 1)
                transposed_hidden(o, h_e[:, t % 2], P).then_inc(S["units"], 1)
                pe.wait_ge(S["sh_t"], t + 1)
                for half in range(2):
                    o = pe_unit(pe, f"sd{t}{half}")
                    down(o, heT[:, t % 2], ws_dn, half, P).then_inc(S["units"], 1)

            pe.wait_ge(S["ld_rt"], 16)
            for t in range(NT + 1):
                if t < NT:
                    normed_rows(t)
                if t:
                    router_logits(t - 1)
            pe.wait_ge(S["ld_sgu"], 32)
            pe.wait_ge(S["ld_sdn"], 16)
            for t in range(NT - 1):
                shared_gate_up(t)
            pe.wait_ge(S["ro_sel"], 1)
            for q in range(NT):
                for j in range(q + 1):
                    m(ps[:, 7, q * NE:(q + 1) * NE], lower[:] if j == q else ones[:], R[4][:, j],
                      start=j == 0, stop=j == q)
            for j in range(NT):
                last = m(ps[:, 7, NT * NE:(NT + 1) * NE], ones[:], R[4][:, j], start=j == 0, stop=j == NT - 1)
            last.then_inc(S["pos_m"], 1)
            shared_gate_up(NT - 1)
            shared_down(0)


            def slots_of(i, e, u, early=False):
                pe.wait_ge(S["place_v"], i + 1)
                if not early:
                    pe.wait_ge(S["idx_v"], i)
                for t in range(NT):
                    row = meta[:, e, t, :] if isinstance(e, int) else \
                        meta[:, bass.ds(e, 1), t, :].rearrange("p o j -> p (o j)")
                    last = m(ps[0:CAP, 7, 0:META], place[:, i2(u), t], row, start=t == 0, stop=t == NT - 1)
                last.then_inc(S["idxm"], 1)

            def rows_t(i, u, gathers, early=False):
                pe.wait_ge(X_GA[u % SLOTS], gathers)
                if not early:
                    pe.wait_ge(S["xt_e"], i)
                xv = xg[0:CAP, u % SLOTS].rearrange("p (c k) -> p k c", k=KD)
                for k in range(KD):
                    last = nc.tensor.transpose(ps[:, k // 4, (k % 4) * CAP:(k % 4 + 1) * CAP], xv[:, k],
                                               ident[0:CAP, 0:CAP])
                last.then_inc(S["xt_m"], 1)

            def gate_up(i, u, loads, early=False):
                pe.wait_ge(S["xt_e"], i + 1)
                if not early:
                    pe.wait_ge(S["h_v"], i - 1)
                pe.wait_ge(W_GU[u], loads)
                for k in range(KD):
                    last = m(ps[0:CAP, 2 + i2(u), :], xgT[:, i2(u), k * CAP:(k + 1) * CAP], w_gu[u][:, :, k],
                             start=k == 0, stop=k == KD - 1)
                last.then_inc(S["gu_m"], 1)

            def hidden_t(i, u, early=False):
                pe.wait_ge(S["h_v"], i + 1)
                if not early:
                    pe.wait_ge(S["ht_a"], i)
                transposed_hidden(ps[:, 4, :], h_e[0:CAP, i2(u)], CAP).then_inc(S["ht_m"], 1)

            def down_rows(i, u, loads, early=False):
                pe.wait_ge(S["ht_a"], i + 1)
                if not early:
                    pe.wait_ge(S["y_a"], i)
                    pe.wait_ge(S["y_v"], i)
                pe.wait_ge(W_DN[u], loads)
                for half in range(2):
                    last = down(ps[0:CAP, 5 + half, :], heT_x[:, i2(u)], w_dn[u], half, CAP)
                last.then_inc(S["dn_m"], 1)

            def group(i0, n, e0, e_next, first=False, last=False):
                for u in range(SLOTS):
                    if not (last and u == SLOTS - 1):
                        rows_t(i0 + (u + 1), u + 1, (n + (u + 1) // SLOTS + 1) * 16)
                    prev = n if u else n - 1
                    if not (first and u == 0):
                        hidden_t(i0 + (u - 1), u + 3, first and u == 1)
                    if not (last and u >= 1):
                        slots_of(i0 + (u + 3), (e_next if u else e0) + (u + 3) % SLOTS, u + 3)
                    gate_up(i0 + u, u, (n + 1) * 32, first and u < 2)
                    if not (first and u == 0):
                        down_rows(i0 + (u - 1), (u + 3) % 4, (prev + 1) * 16, first and u == 1)

            slots_of(0, 0, 0, True)
            shared_down(1)
            slots_of(1, 1, 1)
            shared_down(2)
            slots_of(2, 2, 2)
            shared_down(3)
            pe.wait_ge(S["nch_ready"], 1)
            n_mid = pe.value_load(n_int[0:1, 0:1], min_val=GROUPS - 2, max_val=GROUPS * MAXC - 2)
            pe.wait_ge(S["sh_y"], 2 * NT)
            rows_t(0, 0, 16, True)
            group(0, 0, 0, SLOTS, first=True)
            group(SLOTS, 1, SLOTS, 2 * SLOTS)
            with pe.Fori(2, n_mid + 1) as n:
                group(pe.snap(n * SLOTS), n, pe.snap((n % GROUPS) * SLOTS), pe.snap(((n + 1) % GROUPS) * SLOTS))
            n_last = pe.snap(n_mid + 1)
            i0 = pe.snap(n_last * SLOTS)
            group(i0, n_last, NE - SLOTS, None, last=True)
            hidden_t(i0 + 3, 3)
            down_rows(i0 + 3, 3, (n_last + 1) * 16)


_INS = ["x", "w_in", "hg_lb_logits", "hg_norm_g", "q_norm_g", "w_q_up", "w_qidx_up", "kv_norm_g", "w_kv_up",
        "idx_ln_g", "idx_ln_b", "w_out", "ln1_g", "ln1_b", "w_router", "router_bias", "w_e_gate", "w_e_up",
        "w_e_down", "w_s_gate", "w_s_up", "w_s_down", "ln2_g", "ln2_b"]


def kernel(**inputs):
    import numpy as _np
    import concourse.bacc as _bacc
    from concourse.bass_utils import run_bass_kernel_spmd as _run

    nc = _bacc.Bacc("TRN2", target_bir_lowering=False, num_devices=1)
    arrays, args = {}, []
    for name in _INS:
        a = _np.ascontiguousarray(inputs[name])
        arrays[f"in_{name}"] = a
        args.append(nc.dram_tensor(f"in_{name}", a.shape, mybir.dt.from_np(a.dtype), kind="ExternalInput").ap())
    args.append(nc.dram_tensor("out_0", (1, SEQ, DM), F32, kind="ExternalOutput").ap())
    hybrid_block(nc, *args)
    r = _run(nc, [arrays], core_ids=[0])
    return r.results[0]["out_0"]
```
